# Optimizing a Trainium2 kernel written in Bass

```python
import jax, jax.numpy as jnp
from jax import lax
import numpy as np

D_MODEL = 1024
BATCH = 1
SEQ = 2048
DEPTH = 1

CHUNK = 64
HEAD_DIM = 64
RMS_EPS = 1e-6
NEG_INF = -1e30

A_HEADS = 8
A_WIDTH = A_HEADS * HEAD_DIM
A_LEFT_CHUNKS = 8
A_BAND = (A_LEFT_CHUNKS + 1) * CHUNK
REL_CLIP = 256
REL_TABLE = 2 * REL_CLIP + 1

B_Q_HEADS = 8
B_KV_HEADS = 2
B_GROUP = B_Q_HEADS // B_KV_HEADS
B_WIDTH = B_Q_HEADS * HEAD_DIM
B_KV_WIDTH = B_KV_HEADS * HEAD_DIM
B_WINDOW = 128
B_WINDOW_CHUNKS = B_WINDOW // CHUNK
B_BAND = B_WINDOW_CHUNKS * CHUNK

N_BRANCHES = 2
IN_WIDTHS = (A_WIDTH, A_WIDTH, A_WIDTH, A_WIDTH,
             B_WIDTH, B_KV_WIDTH, B_KV_WIDTH, B_WIDTH,
             N_BRANCHES * D_MODEL)
IN_COLS = int(sum(IN_WIDTHS))
IN_SPLITS = [int(v) for v in np.cumsum(IN_WIDTHS)[:-1]]
ATTN_SCALE = HEAD_DIM ** -0.5

kernel_name = "hybrid_chunked_relbias_swa_sink_gated"

def rms_norm(x, g):
    xf = x.astype(jnp.float32)
    y = xf * lax.rsqrt(jnp.mean(xf * xf, axis=-1, keepdims=True) + RMS_EPS)
    return (y * g.astype(jnp.float32)).astype(x.dtype)

def chunk_band(t, n_left):
    b, s = t.shape[:2]
    nc = s // CHUNK
    tc = t.reshape((b, nc, CHUNK) + t.shape[2:])
    pad = [(0, 0), (n_left, 0)] + [(0, 0)] * (tc.ndim - 2)
    tp = jnp.pad(tc, pad)
    return jnp.concatenate([tp[:, j:j + nc] for j in range(n_left + 1)], axis=2)

def band_valid(nc, n_left):
    c = jnp.arange(nc)[:, None]
    j = jnp.arange(n_left + 1)[None, :]
    return jnp.repeat((c - n_left + j) >= 0, CHUNK, axis=1)

def alibi_slopes(n):
    start = 2.0 ** (-8.0 / n)
    return np.asarray([start ** (h + 1) for h in range(n)], dtype=np.float32)

def chunked_relbias_attention(q, k, v, rel_bias):
    b, s, h, d = q.shape
    nc = s // CHUNK
    qc = q.reshape(b, nc, CHUNK, h, d)
    kb = chunk_band(k, A_LEFT_CHUNKS)
    vb = chunk_band(v, A_LEFT_CHUNKS)
    scores = jnp.einsum('bnqhd,bnkhd->bhnqk', qc, kb,
                        preferred_element_type=jnp.float32) * ATTN_SCALE
    dist = np.arange(CHUNK)[:, None] + A_LEFT_CHUNKS * CHUNK - np.arange(A_BAND)[None, :]
    idx = np.clip(dist, -REL_CLIP, REL_CLIP) + REL_CLIP
    bias = rel_bias.astype(jnp.float32)[:, idx]
    scores = scores + bias[:, None]
    valid = band_valid(nc, A_LEFT_CHUNKS)
    scores = jnp.where(valid[None, None, :, None, :], scores, NEG_INF)
    p = jax.nn.softmax(scores, axis=-1)
    out = jnp.einsum('bhnqk,bnkhd->bnqhd', p.astype(v.dtype), vb)
    return out.reshape(b, s, h * d)

def sliding_window_gqa_sinks(q, k, v, sinks):
    b, s, hq, d = q.shape
    nc = s // CHUNK
    qc = q.reshape(b, nc, CHUNK, B_KV_HEADS, B_GROUP, d)
    kb = chunk_band(k, B_WINDOW_CHUNKS - 1)
    vb = chunk_band(v, B_WINDOW_CHUNKS - 1)
    scores = jnp.einsum('bnqkgd,bnskd->bkgnqs', qc, kb,
                        preferred_element_type=jnp.float32) * ATTN_SCALE
    slopes = jnp.asarray(alibi_slopes(B_Q_HEADS)).reshape(B_KV_HEADS, B_GROUP)
    dist = np.abs(np.arange(CHUNK)[:, None] + (B_WINDOW_CHUNKS - 1) * CHUNK
                  - np.arange(B_BAND)[None, :]).astype(np.float32)
    scores = scores - slopes[:, :, None, None, None] * jnp.asarray(dist)
    valid = band_valid(nc, B_WINDOW_CHUNKS - 1)
    scores = jnp.where(valid[None, None, None, :, None, :], scores, NEG_INF)
    sink = sinks.astype(jnp.float32).reshape(B_KV_HEADS, B_GROUP)[None, :, :, None, None, None]
    m = jnp.maximum(jnp.max(scores, axis=-1, keepdims=True), sink)
    e = jnp.exp(scores - m)
    p = e / (jnp.sum(e, axis=-1, keepdims=True) + jnp.exp(sink - m))
    out = jnp.einsum('bkgnqs,bnskd->bnqkgd', p.astype(v.dtype), vb)
    return out.reshape(b, s, hq * d)

def hybrid_layer(x, g_pre, w_in, rel_bias, sinks, w_branch_a, w_branch_b, w_out, g_post):
    b, s, _ = x.shape
    h = rms_norm(x, g_pre)
    proj = h @ w_in
    qa, ka, va, za, qb, kb, vb, zb, gl = jnp.split(proj, IN_SPLITS, axis=-1)
    ya = chunked_relbias_attention(qa.reshape(b, s, A_HEADS, HEAD_DIM),
                                   ka.reshape(b, s, A_HEADS, HEAD_DIM),
                                   va.reshape(b, s, A_HEADS, HEAD_DIM), rel_bias)
    ya = ya * jax.nn.silu(za)
    yb = sliding_window_gqa_sinks(qb.reshape(b, s, B_Q_HEADS, HEAD_DIM),
                                  kb.reshape(b, s, B_KV_HEADS, HEAD_DIM),
                                  vb.reshape(b, s, B_KV_HEADS, HEAD_DIM), sinks)
    yb = yb * jax.nn.silu(zb)
    gates = jax.nn.sigmoid(gl.astype(jnp.float32)).astype(x.dtype).reshape(b, s, N_BRANCHES, D_MODEL)
    merged = gates[:, :, 0] * (ya @ w_branch_a) + gates[:, :, 1] * (yb @ w_branch_b)
    out = merged @ w_out
    return x + rms_norm(out, g_post)

def setup_inputs(seed: int = 0) -> dict:
    key = jax.random.key(seed)
    ks = jax.random.split(key, 10)
    f32 = jnp.float32
    x = jax.random.normal(ks[0], (BATCH, SEQ, D_MODEL), f32)
    g_pre = 1.0 + 0.05 * jax.random.normal(ks[1], (DEPTH, D_MODEL), f32)
    w_in = jax.random.normal(ks[2], (DEPTH, D_MODEL, IN_COLS), f32) * D_MODEL ** -0.5
    rel_bias = 0.1 * jax.random.normal(ks[3], (DEPTH, A_HEADS, REL_TABLE), f32)
    sinks = 0.5 * jax.random.normal(ks[4], (DEPTH, B_Q_HEADS), f32)
    w_branch_a = jax.random.normal(ks[5], (DEPTH, A_WIDTH, D_MODEL), f32) * A_WIDTH ** -0.5
    w_branch_b = jax.random.normal(ks[6], (DEPTH, B_WIDTH, D_MODEL), f32) * B_WIDTH ** -0.5
    w_out = jax.random.normal(ks[7], (DEPTH, D_MODEL, D_MODEL), f32) * D_MODEL ** -0.5
    g_post = 1.0 + 0.05 * jax.random.normal(ks[8], (DEPTH, D_MODEL), f32)
    return {"x": x, "g_pre": g_pre, "w_in": w_in, "rel_bias": rel_bias, "sinks": sinks,
            "w_branch_a": w_branch_a, "w_branch_b": w_branch_b, "w_out": w_out,
            "g_post": g_post}

def reference(x, g_pre, w_in, rel_bias, sinks, w_branch_a, w_branch_b, w_out, g_post):
    for l in range(DEPTH):
        x = hybrid_layer(x, g_pre[l], w_in[l], rel_bias[l], sinks[l],
                         w_branch_a[l], w_branch_b[l], w_out[l], g_post[l])
    return x


_drawn_inputs = setup_inputs


def setup_inputs(seed=0):
    import zlib

    import numpy as np

    out = dict(_drawn_inputs(seed))
    spreads = {}
    factors = {'rel_bias': 2.778, 'sinks': 4.803}
    for name, (base, spread) in spreads.items():
        noise = np.random.default_rng([zlib.crc32(name.encode()), seed]).standard_normal(out[name].shape)
        drawn = base * np.exp(spread * noise) if base else spread * noise
        out[name] = __import__('jax').numpy.asarray(drawn.astype(out[name].dtype))
    for name, factor in factors.items():
        out[name] = (out[name] * factor).astype(out[name].dtype)
    return out
```

```python
from contextlib import ExitStack

import concourse.bass as bass
from concourse import mybir

F32 = mybir.dt.float32
F32R = mybir.dt.float32r
ALU = mybir.AluOpType
ACT = mybir.ActivationFunctionType
AX = mybir.AxisListType

P = 128
D = 1024
KT = D // P
HD = 64
CHUNK = 64
NH = 8
HP = NH // 2
BLK = 512
TT = BLK // P
A_TILES = 5
A_KEYS = A_TILES * P
B_KEYS = 3 * CHUNK
REL = 513
REL_ROW = A_KEYS + P
REL_NEAR = REL_ROW - (A_KEYS - 1 - REL // 2)
EPS = 1e-6
MASKED = -1e30
FAR = 1e33
C_QA, C_KA, C_VA, C_ZA, C_QB, C_KB, C_VB, C_ZB, C_G = 0, 512, 1024, 1536, 2048, 2560, 2688, 2816, 3328

U_VA, U_KB, U_VB, U_KA, U_ZA, U_ZB, U_QA, U_QB, U_G, U_M, U_O, UNITS = 0, 4, 5, 6, 10, 14, 18, 22, 26, 42, 50, 58
T_GROUPS = (C_KA, C_ZA, C_ZB, C_QA, C_QB)
STEPS = TT * HP

BANK_VA = (4, 0, 5, 1)
BANK_KB, BANK_VB = 6, 2
BANK_T = (7, 3)
BANK_PT = (4, 5)
BANK_Y, BANK_G = 6, 7


def slot_fill(u):
    order = [(U_VA, 0, 1), (U_VA + 2, 1, 1), (U_KB, 0, 1)]
    for u0 in range(U_KA, UNITS, 4):
        n = 2 if U_M <= u0 < U_O else 1
        order += [(u0, 0, n), (u0 + 2, 1, n)]
    count = [0, 0]
    for first, slot, n in order:
        count[slot] += n
        if first <= u < first + 2:
            return slot, count[slot]
    return count


FILLS = slot_fill(UNITS)


def build_block(nc, x, g_pre, w_in, rel_bias, sinks, w_branch_a, w_branch_b, w_out, g_post, out):
    S = x.shape[1]
    NB = S // BLK
    x_v = x.rearrange("a (b t p) d -> a b p t d", p=P, t=TT)[0]
    out_v = out.rearrange("a (b t p) d -> a b p t d", p=P, t=TT)[0]
    w_in_v = w_in[0].rearrange("(k p) c -> p k c", p=P)
    wa_v = w_branch_a[0].rearrange("(k p) c -> p k c", p=P)
    wb_v = w_branch_b[0].rearrange("(k p) c -> p k c", p=P)
    w_out_v = w_out[0].rearrange("(k p) c -> p k c", p=P)
    rel_rows = nc.dram_tensor("rel_rows", (NH, P, REL_ROW), F32, kind="Internal").ap()

    with ExitStack() as ctx:
        def sb(name, shape, dt=F32):
            return ctx.enter_context(nc.sbuf_tensor(name, shape, dt))

        def sem(name):
            return ctx.enter_context(nc.semaphore(name))

        act_hi = sb("act_hi", [P, KT, BLK], F32R)
        act_lo = sb("act_lo", [P, KT, BLK], F32R)
        zx = sb("zx", [P, KT, BLK])
        x_rows = zx[:, :, :].rearrange("p k n -> p (k n)").rearrange("p (t d) -> p t d", t=TT)
        gates_at = -(-nc.sbuf_base // 32) * 32
        gates = sb("gates", [P, 2 * KT, BLK])
        m_parts = nc.alloc_sbuf_tensor_at("m_parts", [P, 2 * KT, BLK], F32R, offset=gates_at)
        q = sb("q", [P, 2 * HP, BLK])
        res_rows = q[:, :, :].rearrange("p k n -> p (k n)").rearrange("p (t d) -> p t d", t=TT)
        k_a = sb("k_a", [P, HP, 2 * BLK])
        v_a = sb("v_a", [P, 2 * TT, NH * HD])
        k_b = sb("k_b", [P, HD + BLK])
        v_b = sb("v_b", [P, TT, 2 * HD])
        v_bh = sb("v_bh", [P, TT + 1, 2 * HD])
        bias_a = sb("bias_a", [P, NH, A_KEYS])
        dist_b = sb("dist_b", [P, B_KEYS])
        w_raw = sb("w_raw", [P, 2, 2048])
        w_hi = sb("w_hi", [P, 2, 1024], F32R)
        w_lo = sb("w_lo", [P, 2, 1024], F32R)
        pa = sb("pa", [P, 2, A_KEYS])
        pb = sb("pb", [P, 2, 2 * P])
        y_rows = sb("y_rows", [P, 2 * NH * HD])
        gpost = sb("gpost", [P, D])
        gpre = sb("gpre", [P, KT])
        ident = sb("ident", [P, P])
        sink = sb("sink", [P, 2, HP])
        nsink = sb("nsink", [P, 2, HP])
        rmax = sb("rmax", [P, 4])
        nmax = sb("nmax", [P, 4])
        rsum = sb("rsum", [P, 4])
        rinv = sb("rinv", [P, 4])
        esink = sb("esink", [P, 2])
        ssq = sb("ssq", [P, 2, TT])
        mhalf = sb("mhalf", [P, TT])
        var = sb("var", [P, TT])
        r0 = sb("r0", [P, TT])
        r1 = sb("r1", [P, TT])
        rstd = sb("rstd", [P, TT])
        ps = ctx.enter_context(nc.psum_tensor("ps", [P, 8, 512], F32))
        scores = [ps[:, 2 * j:2 * j + 2, :].rearrange("p b n -> p (b n)") for j in range(2)]
        hi_r, lo_r = m_parts[:, 0:KT, :], m_parts[:, KT:2 * KT, :]

        def cols(w, slot):
            return w[:, slot, :].rearrange("p (k c) -> p k c", k=KT)

        def rows(w, slot):
            return w[:, slot, :].rearrange("p (k c) -> p k c", k=2)

        def as_f32(ap):
            return ap.bitcast(F32)

        def scaled_rows(t):
            return pa[:, :, :].rearrange("p j n -> p (j n)")[:, 0:D] if t % 2 == 0 else y_rows[:, :]

        def raw_cols(slot, half):
            return w_raw[:, slot, :].rearrange("p (k c) -> p k c", k=KT)[:, :, half * P:half * P + P]

        def raw_unit(u):
            slot, _ = slot_fill(u)
            half = u % 2
            if u < U_KB or u >= U_O:
                return w_raw[:, slot, half * 1024:half * 1024 + 1024]
            return raw_cols(slot, half)

        def part_unit(w, u):
            if u < U_KB or u >= U_O:
                return w[:, u % 2, :]
            return cols(w, u % 2)

        raw_full = [sem("raw_full0"), sem("raw_full1")]
        hi_ready = sem("hi_ready")
        lo_ready = sem("lo_ready")
        unit_done = sem("unit_done")
        x_full = sem("x_full")
        sq_done = sem("sq_done")
        var_x = sem("var_x")
        pow_done = sem("pow_done")
        newton = sem("newton")
        h_ready = sem("h_ready")
        turned = sem("turned")
        hT_hi = sem("hT_hi")
        hT_lo = sem("hT_lo")
        tanh_done = sem("tanh_done")
        proj_read = sem("proj_read")
        shifted = sem("shifted")
        qk_done = sem("qk_done")
        biased_b = sem("biased_b")
        nmax_a = sem("nmax_a")
        scores_read = sem("scores_read")
        max_b = sem("max_b")
        nmax_b = sem("nmax_b")
        sink_arg = sem("sink_arg")
        exp_a = sem("exp_a")
        exp_b = sem("exp_b")
        exp_sink = sem("exp_sink")
        sum_b = sem("sum_b")
        inv_ready = sem("inv_ready")
        turn = [sem(f"turn{i}") for i in range(4)]
        pt_ready = [sem(f"pt_ready{i}") for i in range(4)]
        pv_done = sem("pv_done")
        y_ready = sem("y_ready")
        yt_done = sem("yt_done")
        yt_read = sem("yt_read")
        gate_read = sem("gate_read")
        yT_hi = sem("yT_hi")
        yT_lo = sem("yT_lo")
        merge_read = sem("merge_read")
        m_sum = sem("m_sum")
        m_hi = sem("m_hi")
        m_lo = sem("m_lo")
        out_sq = sem("out_sq")
        sq_sum = sem("sq_sum")
        var_o = sem("var_o")
        scaled = sem("scaled")
        added = sem("added")
        res_full = sem("res_full")
        stored = sem("stored")
        ready = {n: sem(f"c_{n}") for n in ("dma", "ident0", "ident", "dist0", "dist1", "rel", "relrow", "relst",
                                            "bias", "mask", "nsink", "mhalf")}

        block = ctx.enter_context(nc.Block())

        @block.sync
        def _(sp):
            def pair(slot, srcs, b, before, first):
                if before is not None:
                    sp.wait_ge(hi_ready, b * UNITS + before)
                    sp.wait_ge(lo_ready, b * UNITS + before)
                for dst, src in srcs(w_raw[:, slot, :]):
                    sp.dma_start(dst, src).then_inc(raw_full[slot], 16)

            def w_cols(c):
                return lambda raw: [(raw.rearrange("p (k c) -> p k c", k=KT), w_in_v[:, :, c])]

            def w_rows(src, k, c):
                return lambda raw: [(raw.rearrange("p (k c) -> p k c", k=4), src[:, k:k + 4, c:c + 512])]

            def w_branches(c):
                def srcs(raw):
                    v = raw.rearrange("p (k c) -> p k c", k=KT)
                    return [(v[:, 0:4, :], wa_v[:, :, c]), (v[:, 4:8, :], wb_v[:, :, c])]
                return srcs

            def store_rows(b):
                for t in range(TT):
                    sp.wait_ge(added, b * TT + t + 1)
                    sp.dma_start(out_v[b][:, t, :], res_rows[:, t, :]).then_inc(stored, 16)

            def body(b, first):
                if not first:
                    sp.wait_ge(yT_hi, b * KT)
                    sp.wait_ge(yT_lo, b * KT)
                sp.dma_start(x_rows, x_v[b]).then_inc(x_full, 16)
                pair(0, w_rows(w_in_v, 0, C_VA), b, None if first else -2, first)
                pair(1, w_rows(w_in_v, 4, C_VA), b, None if first else 0, first)
                if not first:
                    store_rows(b - 1)
                pair(0, w_cols(slice(C_KB, C_KB + 256)), b, U_VA + 2, first)
                for n, c in enumerate(T_GROUPS):
                    u0 = U_KA + 4 * n
                    pair(0, w_cols(slice(c, c + 256)), b, u0 - 2 if n else U_KA, first)
                    pair(1, w_cols(slice(c + 256, c + 512)), b, u0 if n else U_KB, first)
                with sp.Fori(0, 4) as i:
                    bb = b * UNITS + i * 4 + U_G
                    for slot in range(2):
                        sp.wait_ge(hi_ready, bb + (2 * slot - 2))
                        sp.wait_ge(lo_ready, bb + (2 * slot - 2))
                        sp.dma_start(w_raw[:, slot, :].rearrange("p (k c) -> p k c", k=KT),
                                     w_in_v[:, :, bass.ds(i * 512 + (C_G + 256 * slot), 256)]).then_inc(raw_full[slot], 16)
                for u0 in range(U_M, U_O, 4):
                    for slot in range(2):
                        c = 128 * (u0 - U_M + 2 * slot)
                        pair(slot, w_branches(slice(c, c + 256)), b, u0 + 2 * slot - 2, first)
                    if u0 == U_M:
                        sp.wait_ge(qk_done, b * STEPS + STEPS)
                        sp.dma_start(res_rows, x_v[b]).then_inc(res_full, 16)
                for u0 in range(U_O, UNITS, 4):
                    for slot in range(2):
                        pair(slot, w_rows(w_out_v, 4 * slot, 128 * (u0 - U_O)), b, u0 + 2 * slot - 2, first)

            sp.dma_start(pa[0:NH, 0, 0:REL], rel_bias[0]).then_inc(ready["rel"], 16)
            with nc.allow_non_contiguous_dma(reason="1024 words, once"):
                sp.dma_start(gpre[:, :], g_pre[0].rearrange("(k p) -> p k", p=P)).then_inc(ready["dma"], 16)
            sp.dma_start(sink[:, :, :].rearrange("p j i -> p (j i)"), sinks[0:1, :].broadcast_to([P, NH])).then_inc(ready["dma"], 16)
            sp.dma_start(gpost[:, :], g_post[0:1, :].broadcast_to([P, D])).then_inc(ready["dma"], 16)
            body(0, True)
            with sp.Fori(1, NB) as b:
                body(b, False)
            store_rows(NB - 1)
            sp.wait_ge(stored, NB * TT * 16)

        @block.gpsimd
        def _(pool):
            def body(b, first):
                pool.wait_ge(var_x, b + 1)
                pool.tensor_tensor(r0[:, :], var[:, :], mhalf[:, :], ALU.pow).then_inc(pow_done, 1)

                pool.wait_ge(var_o, b + 1)
                pool.tensor_tensor(r0[:, :], var[:, :], mhalf[:, :], ALU.pow).then_inc(pow_done, 1)
                pool.wait_ge(res_full, (b + 1) * 16)
                for t in range(TT):
                    pool.wait_ge(scaled, b * TT + t + 1)
                    pool.tensor_tensor(res_rows[:, t, :], res_rows[:, t, :], scaled_rows(t), ALU.add).then_inc(added, 1)

            pool.memset(mhalf[:, :], -0.5).then_inc(ready["mhalf"], 1)
            pool.memset(ident[:, :], 0.0).then_inc(ready["ident0"], 1)
            pool.wait_ge(ready["ident0"], 1)
            pool.affine_select(out=ident[:, :], in_=ident[:, :], compare_op=ALU.not_equal, fill=1.0, base=0,
                               pattern=[[-1, P]], channel_multiplier=1).then_inc(ready["ident"], 1)
            pool.iota(dist_b[:, :], pattern=[[-1, B_KEYS]], base=CHUNK, channel_multiplier=1,
                      allow_small_or_imprecise_dtypes=True).then_inc(ready["dist0"], 1)
            pool.wait_ge(ready["relrow"], 2)
            pool.dma_start(rel_rows, gates[0:NH, 0:2, :].rearrange("h a n -> h (a n)")[:, 0:REL_ROW]
                           .unsqueeze(1).broadcast_to([NH, P, REL_ROW])).then_inc(ready["relst"], 16)
            pool.wait_ge(ready["relst"], 16)
            pool.dma_start(bias_a[:, :, :], bass.AP(
                tensor=rel_rows.tensor, offset=P - 1,
                ap=[[REL_ROW - 1, P], [P * REL_ROW, NH], [1, A_KEYS]])).then_inc(ready["bias"], 16)
            pool.wait_ge(ready["bias"], 16)
            pool.wait_ge(ready["dist1"], 1)
            for n, (place, value) in enumerate([(bias_a[0:HD, :, A_KEYS - CHUNK:A_KEYS], MASKED),
                                                (bias_a[HD:P, :, 0:CHUNK], MASKED),
                                                (dist_b[0:HD, 2 * CHUNK:B_KEYS], FAR),
                                                (dist_b[HD:P, 0:CHUNK], FAR)]):
                if n:
                    pool.wait_ge(ready["mask"], n)
                pool.memset(place, value).then_inc(ready["mask"], 1)
            pool.wait_ge(ready["mask"], 4)
            body(0, True)
            with pool.Fori(1, NB) as b:
                body(b, False)

        @block.scalar
        def _(act):
            def split_hi(b, u, first, loop=0):
                slot, fill = slot_fill(u)
                act.wait_ge(raw_full[slot], b * (16 * FILLS[slot]) + loop * 16 + fill * 16)
                if not (first and u < 2):
                    act.wait_ge(unit_done, b * UNITS + loop * 4 + (u - 1))
                act.activation(part_unit(w_hi, u), raw_unit(u), ACT.Copy).then_inc(hi_ready, 1)

            def body(b, first):
                split_hi(b, 0, first)
                split_hi(b, 1, first)
                act.wait_ge(x_full, b * 16 + 16)
                if not first:
                    act.wait_ge(added, b * TT)
                for t in range(TT):
                    if t:
                        act.wait_ge(sq_done, b * TT + t)
                    act.activation(y_rows[:, :], x_rows[:, t, :], ACT.Square, accum_out=ssq[:, 0, t:t + 1])\
                       .then_inc(sq_done, 1)
                for k in range(KT):
                    act.wait_ge(turned, b * KT + k + 1)
                    act.activation(act_hi[:, k, :], ps[:, k, :], ACT.Copy, scale=gpre[:, k:k + 1]).then_inc(hT_hi, 1)

                for u in range(U_G):
                    if U_ZA <= u < U_QA:
                        act.wait_ge(unit_done, b * UNITS + u + 1)
                        act.activation(zx[:, u - U_ZA, :], ps[:, BANK_T[u % 2], :], ACT.Tanh, scale=0.5)\
                           .then_inc(tanh_done, 1)
                    split_hi(b, u + 2, first)

                def step(t, hp):
                    s = b * STEPS + t * HP + hp
                    n = t + 1 if first else A_TILES
                    nb = 2 * CHUNK if first and t == 0 else B_KEYS
                    act.wait_ge(nmax_a, s + 1)
                    for j in range(2):
                        act.activation(pa[:, j, 0:n * P], pa[:, j, 0:n * P], ACT.Exp, bias=nmax[:, j:j + 1],
                                       accum_out=rsum[:, j:j + 1]).then_inc(exp_a, 1)
                    act.wait_ge(nmax_b, s + 1)
                    for j in range(2):
                        act.activation(pb[:, j, B_KEYS - nb:B_KEYS], pb[:, j, B_KEYS - nb:B_KEYS], ACT.Exp,
                                       bias=nmax[:, 2 + j:3 + j], accum_out=rsum[:, 2 + j:3 + j]).then_inc(exp_b, 1)
                    act.wait_ge(sink_arg, s + 1)
                    act.activation(esink[:, :], esink[:, :], ACT.Exp).then_inc(exp_sink, 1)
                    m = min(n, 4) * P
                    for j in range(2):
                        act.wait_ge(turn[j], s + 1)
                        act.activation(pa[:, j, 0:m], ps[:, BANK_PT[j], 0:m], ACT.Copy).then_inc(pt_ready[j], 1)
                    act.wait_ge(unit_done, b * UNITS + t * HP + (U_G + hp + 1))
                    act.activation(gates[:, bass.ds(t * HP + hp, 1), :].rearrange("p a n -> p (a n)"),
                                   ps[:, BANK_G, :], ACT.Tanh, scale=0.5).then_inc(gate_read, 1)

                if first:
                    for t in range(TT):
                        for hp in range(HP):
                            step(t, hp)
                            split_hi(b, U_G + t * HP + hp + 2, first)
                else:
                    with act.Fori(0, TT - 1) as t:
                        for hp in range(HP):
                            step(t, hp)
                            split_loop(act, b, t, hp)
                    for hp in range(HP):
                        step(TT - 1, hp)
                        split_hi(b, U_G + (TT - 1) * HP + hp + 2, first)

                for k in range(KT):
                    act.wait_ge(yt_read, b * 2 * TT + 2 * TT)
                    act.activation(act_hi[:, k, :], zx[:, k, :], ACT.Copy).then_inc(yT_hi, 1)

                for c in range(KT):
                    act.wait_ge(m_sum, b * KT + c + 1)
                    act.activation(hi_r[:, c, :], pa[:, c % 2, 0:BLK], ACT.Copy).then_inc(m_hi, 1)
                    split_hi(b, U_M + c + 2, first)

                for u in range(U_O, UNITS):
                    if u + 2 < UNITS:
                        split_hi(b, u + 2, first)
                    if u == U_O + 1:
                        act.activation(k_a[:, :, 0:BLK], k_a[:, :, BLK:2 * BLK], ACT.Copy).then_inc(shifted, 1)
                    if u == U_O + 2:
                        act.activation(v_a[:, 0:TT, :], v_a[:, TT:2 * TT, :], ACT.Copy).then_inc(shifted, 1)
                        act.activation(k_b[:, 0:HD], k_b[:, BLK:BLK + HD], ACT.Copy).then_inc(shifted, 1)
                        act.activation(v_bh[0:HD, 0, :], v_bh[0:HD, TT, :], ACT.Copy).then_inc(shifted, 1)
                    if u == U_O + 3:
                        for t in range(TT):
                            act.wait_ge(unit_done, b * UNITS + U_O + 4)
                            square(b, t, 0)
                act.wait_ge(unit_done, b * UNITS + UNITS)
                for t in range(TT):
                    square(b, t, 1)

            def square(b, t, half):
                n = half * TT + t
                if n >= 2:
                    act.wait_ge(out_sq, b * (2 * TT) + (n - 1))
                act.activation(y_rows[:, 512 * (n % 2):512 * (n % 2) + 512], ps[:, t if half else 4 + t, :], ACT.Square,
                               accum_out=ssq[:, half, t:t + 1]).then_inc(out_sq, 1)

            def split_loop(eng, b, t, hp):
                u = U_G + hp + 2
                slot, fill = slot_fill(u)
                eng.wait_ge(raw_full[slot], b * (16 * FILLS[slot]) + t * 16 + fill * 16)
                eng.wait_ge(unit_done, b * UNITS + t * HP + (u - 1))
                eng.activation(part_unit(w_hi, u), raw_unit(u), ACT.Copy).then_inc(hi_ready, 1)

            act.wait_ge(ready["dma"], 48)
            body(0, True)
            with act.Fori(1, NB) as b:
                body(b, False)

        @block.vector
        def _(dve):
            def split_lo(b, u, t=0):
                dve.wait_ge(hi_ready, b * UNITS + t * 4 + (u + 1))
                dve.tensor_tensor(part_unit(w_lo, u), raw_unit(u), as_f32(part_unit(w_hi, u)), ALU.subtract)\
                   .then_inc(lo_ready, 1)

            def refine(n, half):
                dve.wait_ge(pow_done, n + 1)
                dve.tensor_tensor(r1[:, :], r0[:, :], r0[:, :], ALU.mult).then_inc(newton, 1)
                dve.wait_ge(newton, n * 4 + 1)
                dve.tensor_tensor(r1[:, :], r1[:, :], var[:, :], ALU.mult).then_inc(newton, 1)
                dve.wait_ge(newton, n * 4 + 2)
                dve.tensor_scalar(r1[:, :], r1[:, :], -0.5, 1.5, ALU.mult, ALU.add).then_inc(newton, 1)
                dve.wait_ge(newton, n * 4 + 3)
                dve.tensor_tensor(rstd[:, :], r1[:, :], r0[:, :], ALU.mult).then_inc(newton, 1)
                dve.wait_ge(newton, n * 4 + 4)

            def body(b, first):
                split_lo(b, 0)
                split_lo(b, 1)
                dve.wait_ge(sq_done, b * TT + TT)
                dve.tensor_scalar(var[:, :], ssq[:, 0, :], 1.0 / D, EPS, ALU.mult, ALU.add).then_inc(var_x, 1)
                refine(b * 2, 0)
                for t in range(TT):
                    dve.tensor_scalar(x_rows[:, t, :], x_rows[:, t, :], rstd[:, t:t + 1], None, ALU.mult)\
                       .then_inc(h_ready, 1)
                for k in range(KT):
                    dve.wait_ge(hT_hi, b * KT + k + 1)
                    dve.scalar_tensor_tensor(out=act_lo[:, k, :], in0=ps[:, k, :], scalar=gpre[:, k:k + 1],
                                             in1=as_f32(act_hi[:, k, :]), op0=ALU.mult, op1=ALU.subtract)\
                       .then_inc(hT_lo, 1)

                for u in range(U_G):
                    if u >= U_KB:
                        dve.wait_ge(unit_done, b * UNITS + u + 1)
                    bank = ps[:, BANK_T[u % 2], :]
                    if u == U_KB:
                        if not first:
                            dve.wait_ge(shifted, b * 4)
                        dve.tensor_copy(k_b[:, HD:HD + BLK], ps[:, BANK_KB, :]).then_inc(proj_read, 1)
                    elif u == U_VB:
                        if not first:
                            dve.wait_ge(shifted, b * 4)
                        dve.tensor_copy(v_bh[0:HD, 1:TT + 1, :].rearrange("p t c -> p (t c)"), ps[HD:P, BANK_VB, :])
                        dve.tensor_copy(v_b[:, :, :].rearrange("p t c -> p (t c)"), ps[:, BANK_VB, :])\
                           .then_inc(proj_read, 1)
                    elif U_KA <= u < U_ZA:
                        dve.tensor_copy(k_a[:, u - U_KA, BLK:2 * BLK], bank).then_inc(proj_read, 1)
                    elif U_ZA <= u < U_QA:
                        n = u - U_ZA
                        dve.wait_ge(tanh_done, b * KT + n + 1)
                        dve.scalar_tensor_tensor(out=zx[:, n, :], in0=zx[:, n, :], scalar=1.0, in1=bank,
                                                 op0=ALU.add, op1=ALU.mult).then_inc(proj_read, 1)
                    elif U_QA <= u < U_QB:
                        if not first and u == U_QA:
                            dve.wait_ge(stored, b * (16 * TT))
                        dve.tensor_scalar(q[:, u - U_QA, :], bank, HD ** -0.5, None, ALU.mult).then_inc(proj_read, 1)
                    elif U_QB <= u < U_G:
                        n = u - U_QB
                        half = n // 2
                        for i in range(2):
                            o = dve.tensor_scalar(q[HD * half:HD * half + HD, HP + (2 * n + i) % HP, :],
                                                  ps[HD * i:HD * i + HD, BANK_T[u % 2], :], HD ** -0.5, None, ALU.mult)
                        o.then_inc(proj_read, 1)
                    split_lo(b, u + 2)
                    if u == U_VA + 3:
                        dve.wait_ge(unit_done, b * UNITS + u + 1)
                        if not first:
                            dve.wait_ge(shifted, b * 4)
                        for t in range(TT):
                            dve.tensor_copy(v_a[:, TT + t, :], ps[:, BANK_VA[t], :]).then_inc(proj_read, 1)

                def step(t, hp):
                    s = b * STEPS + t * HP + hp
                    n = t + 1 if first else A_TILES
                    b0 = CHUNK if first and t == 0 else 0
                    dve.wait_ge(qk_done, s + 1)
                    for j in range(2):
                        slope = 2.0 ** (-8.0 / NH * (hp + HP * j + 1))
                        dve.scalar_tensor_tensor(out=pb[:, j, b0:B_KEYS], in0=dist_b[:, b0:B_KEYS], scalar=-slope,
                                                 in1=scores[j][:, A_KEYS + b0:A_KEYS + B_KEYS],
                                                 op0=ALU.mult, op1=ALU.add).then_inc(biased_b, 1)
                    for j in range(2):
                        dve.tensor_tensor_reduce(pa[:, j, 0:n * P], scores[j][:, 0:n * P],
                                                 bias_a[:, 2 * hp + j, A_KEYS - n * P:A_KEYS], 1.0, -3e38,
                                                 ALU.add, ALU.max, rmax[:, j:j + 1]).then_inc(scores_read, 1)
                    dve.wait_ge(scores_read, s * 2 + 2)
                    dve.tensor_scalar(nmax[:, 0:2], rmax[:, 0:2], -1.0, None, ALU.mult).then_inc(nmax_a, 1)
                    dve.wait_ge(biased_b, s * 2 + 2)
                    dve.tensor_reduce(rmax[:, 2:4], pb[:, :, b0:B_KEYS], AX.X, ALU.max).then_inc(max_b, 1)
                    dve.wait_ge(max_b, s + 1)
                    dve.scalar_tensor_tensor(out=nmax[:, 2:4], in0=rmax[:, 2:4], scalar=-1.0, in1=nsink[:, :, hp],
                                             op0=ALU.mult, op1=ALU.min).then_inc(nmax_b, 1)
                    dve.wait_ge(nmax_b, s + 1)
                    dve.tensor_tensor(esink[:, :], sink[:, :, hp], nmax[:, 2:4], ALU.add).then_inc(sink_arg, 1)
                    dve.wait_ge(exp_sink, s + 1)
                    dve.tensor_tensor(rsum[:, 2:4], rsum[:, 2:4], esink[:, :], ALU.add).then_inc(sum_b, 1)
                    dve.wait_ge(sum_b, s + 1)
                    dve.reciprocal(rinv[:, :], rsum[:, :]).then_inc(inv_ready, 1)
                    if not first:
                        dve.wait_ge(turn[2], s - STEPS + 1)
                        dve.tensor_copy(pa[:, :, 4 * P:5 * P], ps[:, BANK_PT[0], 0:2 * P].rearrange("p (j n) -> p j n", j=2))\
                           .then_inc(pt_ready[2], 1)
                    dve.wait_ge(turn[3], s + 1)
                    turned_b = ps[:, BANK_PT[1], :].rearrange("p (j n) -> p j n", j=2)
                    if b0 == 0:
                        dve.tensor_copy(pb[0:HD, :, 0:P], turned_b[0:HD, :, 0:P])
                    dve.tensor_copy(pb[:, :, P:2 * P], turned_b[:, :, P:2 * P]).then_inc(pt_ready[3], 1)
                    dve.wait_ge(inv_ready, s + 1)
                    dve.wait_ge(pv_done, s + 1)
                    y_h = y_rows[:, :].rearrange("p (h d) -> p h d", d=HD)
                    acc = ps[:, BANK_Y, 0:4 * HD].rearrange("p (h d) -> p h d", d=HD)
                    dve.tensor_tensor(y_h[:, 2 * hp:2 * hp + 2, :], acc[:, 0:2, :],
                                      rinv[:, 0:2].unsqueeze(2).broadcast_to([P, 2, HD]), ALU.mult)
                    dve.tensor_tensor(y_h[:, NH + hp:NH + hp + HP + 1:HP, :], acc[:, 2:4, :],
                                      rinv[:, 2:4].unsqueeze(2).broadcast_to([P, 2, HD]), ALU.mult).then_inc(y_ready, 1)

                def gate_y(t):
                    for br in range(2):
                        z_t = zx[:, br * HP:br * HP + HP, bass.ds(t * P, P)]
                        dve.wait_ge(yt_done, b * (2 * TT) + t * 2 + (br + 1))
                        dve.tensor_tensor(z_t, ps[:, BANK_PT[br], :].rearrange("p (k n) -> p k n", k=HP), z_t, ALU.mult)\
                           .then_inc(yt_read, 1)

                if first:
                    dve.wait_ge(ready["mask"], 4)
                    for t in range(TT):
                        for hp in range(HP):
                            step(t, hp)
                            if hp == HP - 1:
                                gate_y(t)
                            split_lo(b, U_G + t * HP + hp + 2)
                else:
                    with dve.Fori(0, TT - 1) as t:
                        for hp in range(HP):
                            step(t, hp)
                            if hp == HP - 1:
                                gate_y(t)
                            split_lo(b, U_G + hp + 2, t)
                    for hp in range(HP):
                        step(TT - 1, hp)
                        if hp == HP - 1:
                            gate_y(TT - 1)
                        split_lo(b, U_G + (TT - 1) * HP + hp + 2)

                for k in range(KT):
                    dve.wait_ge(yT_hi, b * KT + k + 1)
                    dve.tensor_tensor(act_lo[:, k, :], zx[:, k, :], as_f32(act_hi[:, k, :]), ALU.subtract)\
                       .then_inc(yT_lo, 1)

                b_side = pb[:, :, :].rearrange("p j n -> p (j n)")
                for c in range(KT):
                    m = pa[:, c % 2, 0:BLK]
                    dve.wait_ge(unit_done, b * UNITS + U_M + c + 1)
                    dve.scalar_tensor_tensor(out=m, in0=gates[:, c, :], scalar=1.0, in1=ps[:, 2 * (c % 2), :],
                                             op0=ALU.add, op1=ALU.mult)
                    dve.scalar_tensor_tensor(out=b_side, in0=gates[:, KT + c, :], scalar=1.0,
                                             in1=ps[:, 2 * (c % 2) + 1, :], op0=ALU.add, op1=ALU.mult)\
                       .then_inc(merge_read, 1)
                    dve.wait_ge(merge_read, b * KT + c + 1)
                    dve.tensor_tensor(m, m, b_side, ALU.add).then_inc(m_sum, 1)
                    split_lo(b, U_M + c + 2)
                    dve.wait_ge(m_hi, b * KT + c + 1)
                    dve.tensor_tensor(lo_r[:, c, :], m, as_f32(hi_r[:, c, :]), ALU.subtract).then_inc(m_lo, 1)

                for u in range(U_O, UNITS - 2):
                    split_lo(b, u + 2)
                dve.wait_ge(out_sq, (b + 1) * (2 * TT))
                dve.tensor_tensor(ssq[:, 0, :], ssq[:, 0, :], ssq[:, 1, :], ALU.add).then_inc(sq_sum, 1)
                dve.wait_ge(sq_sum, b + 1)
                dve.tensor_scalar(var[:, :], ssq[:, 0, :], 1.0 / D, 16 * EPS, ALU.mult, ALU.add).then_inc(var_o, 1)
                refine(b * 2 + 1, 1)
                for t in range(TT):
                    if t >= 2:
                        dve.wait_ge(added, b * TT + t - 1)
                    for half in range(2):
                        o = dve.scalar_tensor_tensor(out=scaled_rows(t)[:, half * 512:half * 512 + 512],
                                                     in0=ps[:, 4 + t if half == 0 else t, :], scalar=rstd[:, t:t + 1],
                                                     in1=gpost[:, half * 512:half * 512 + 512],
                                                     op0=ALU.mult, op1=ALU.mult)
                    o.then_inc(scaled, 1)

            dve.wait_ge(ready["dma"], 48)
            dve.tensor_scalar(nsink[:, :, :], sink[:, :, :], -1.0, None, ALU.mult).then_inc(ready["nsink"], 1)
            far = REL_ROW - REL_NEAR
            rel_row = gates[0:NH, 0:2, :].rearrange("p a n -> p (a n)")
            dve.wait_ge(ready["rel"], 16)
            dve.tensor_copy(rel_row[:, 0:far], pa[0:NH, 0, REL - 1:REL].broadcast_to([NH, far])).then_inc(ready["relrow"], 1)
            dve.tensor_copy(rel_row[:, far:REL_ROW], pa[0:NH, 0, REL - REL_NEAR:REL][:, ::-1]).then_inc(ready["relrow"], 1)
            dve.wait_ge(ready["dist0"], 1)
            dve.scalar_tensor_tensor(out=dist_b[:, :], in0=dist_b[:, :], scalar=-1.0, in1=dist_b[:, :],
                                     op0=ALU.mult, op1=ALU.max).then_inc(ready["dist1"], 1)
            body(0, True)
            with dve.Fori(1, NB) as b:
                body(b, False)

        @block.tensor
        def _(pe):
            def three(out_ap, lhs, rhs, start, stop):
                (lh, ll), (rh, rl) = lhs, rhs
                pe.matmul(out_ap, lh, rh, start=start, stop=False)
                pe.matmul(out_ap, lh, rl, start=False, stop=False)
                return pe.matmul(out_ap, ll, rh, start=False, stop=stop)

            def w_tile(slot, k):
                return cols(w_hi, slot)[:, k, :], cols(w_lo, slot)[:, k, :]

            def w_row(slot, k):
                return rows(w_hi, slot)[:, k, :], rows(w_lo, slot)[:, k, :]

            def a_cols(k):
                return act_hi[:, k, :], act_lo[:, k, :]

            def a_tile(k, t):
                return act_hi[:, k, t * P:t * P + P], act_lo[:, k, t * P:t * P + P]

            def m_tile(k, t):
                return hi_r[:, k, t * P:t * P + P], lo_r[:, k, t * P:t * P + P]

            def body(b, first):
                if not first:
                    pe.wait_ge(scaled, b * TT)
                pe.wait_ge(h_ready, b * TT + TT)
                for k in range(KT):
                    for t in range(TT):
                        m = pe.transpose(ps[:, k, t * P:t * P + P], x_rows[:, t, k * P:k * P + P], ident[:, :])
                    m.then_inc(turned, 1)

                pe.wait_ge(hT_lo, b * KT + KT)
                for u in range(U_VA, U_KB):
                    pe.wait_ge(lo_ready, b * UNITS + u + 1)
                    for t in range(TT):
                        for i in range(2):
                            k = 2 * u + i
                            m = three(ps[:, BANK_VA[t], :], a_tile(k, t), w_row(u % 2, i), k == 0, k == KT - 1)
                    m.then_inc(unit_done, 1)
                pe.wait_ge(lo_ready, b * UNITS + U_KB + 1)
                for k in range(KT):
                    m = three(ps[:, BANK_KB, :], w_tile(U_KB % 2, k), a_cols(k), k == 0, k == KT - 1)
                m.then_inc(unit_done, 1)
                pe.wait_ge(lo_ready, b * UNITS + U_VB + 1)
                for t in range(TT):
                    for k in range(KT):
                        m = three(ps[:, BANK_VB, t * P:t * P + P], a_tile(k, t), w_tile(U_VB % 2, k), k == 0, k == KT - 1)
                m.then_inc(unit_done, 1)
                with pe.Fori(0, (U_G - U_KA) // 2) as i:
                    for j in range(2):
                        u = b * UNITS + i * 2 + (U_KA + j)
                        pe.wait_ge(lo_ready, u + 1)
                        pe.wait_ge(proj_read, b * 26 + i * 2 + (U_KA + j - 1))
                        for k in range(KT):
                            m = three(ps[:, BANK_T[j], :], w_tile(j, k), a_cols(k), k == 0, k == KT - 1)
                        m.then_inc(unit_done, 1)

                def gate_part(hp, ks):
                    for k in ks:
                        m = three(ps[:, BANK_G, :], w_tile(hp % 2, k), a_cols(k), k == 0, k == KT - 1)
                    return m

                def step(t, hp):
                    s = b * STEPS + t * HP + hp
                    n = t + 1 if first else A_TILES
                    whole = not (first and t == 0)
                    start = (first and t == 0 and hp == 0)
                    k0 = (TT + t - (n - 1)) * P
                    if not start:
                        pe.wait_ge(scores_read, s * 2)
                    for j in range(2):
                        rows_j = slice(HD * j, HD * j + HD)
                        q_a, q_b = q[rows_j, hp, t * P:t * P + P], q[rows_j, HP + hp, t * P:t * P + P]
                        m1 = min(n, 4) * P
                        pe.matmul(scores[j][:, 0:m1], q_a, k_a[rows_j, hp, k0:k0 + m1], start=True, stop=True)
                        if n == A_TILES:
                            pe.matmul(scores[j][:, 4 * P:5 * P], q_a, k_a[rows_j, hp, k0 + 4 * P:k0 + 5 * P],
                                      start=True, stop=True)
                        if whole:
                            m = pe.matmul(scores[j][:, A_KEYS:A_KEYS + B_KEYS], q_b,
                                          k_b[rows_j, t * P:t * P + B_KEYS], start=True, stop=True)
                        else:
                            m = pe.matmul(scores[j][:, A_KEYS + CHUNK:A_KEYS + B_KEYS], q_b,
                                          k_b[rows_j, CHUNK:CHUNK + P], start=True, stop=True)
                    m.then_inc(qk_done, 1)

                    pe.wait_ge(lo_ready, b * UNITS + t * HP + (U_G + hp + 1))
                    if not start:
                        pe.wait_ge(gate_read, s)
                    gate_part(hp, range(0, 4))

                    for j in range(2):
                        pe.wait_ge(exp_a, s * 2 + (j + 1))
                        if hp == 0 and not start:
                            pe.wait_ge(yt_read, b * (2 * TT) + t * 2 - (1 - j))
                        for i in range(min(n, 4)):
                            m = pe.transpose(ps[:, BANK_PT[j], i * P:i * P + P], pa[:, j, i * P:i * P + P], ident[:, :])
                        m.then_inc(turn[j], 1)
                    gate_part(hp, range(4, 5))
                    pe.wait_ge(pt_ready[0], s + 1)
                    if n == A_TILES:
                        for j in range(2):
                            m = pe.transpose(ps[:, BANK_PT[0], j * P:j * P + P], pa[:, j, 4 * P:5 * P], ident[:, :])
                        m.then_inc(turn[2], 1)
                    pe.wait_ge(pt_ready[1], s + 1)
                    pe.wait_ge(exp_b, s * 2 + 2)
                    for j in range(2):
                        m = pe.transpose(ps[:, BANK_PT[1], (2 * j + 1) * P:(2 * j + 2) * P], pb[:, j, CHUNK:B_KEYS],
                                         ident[:, :])
                        if whole:
                            m = pe.transpose(ps[0:CHUNK, BANK_PT[1], 2 * j * P:2 * j * P + P], pb[:, j, 0:CHUNK],
                                             ident[:, :])
                    m.then_inc(turn[3], 1)
                    gate_part(hp, range(5, 7))

                    if not start:
                        pe.wait_ge(y_ready, s)
                    v0 = TT + t - (n - 1)
                    if n == A_TILES:
                        pe.wait_ge(pt_ready[2], s - STEPS + 1)
                    for j in range(2):
                        for i in range(n):
                            pe.matmul(ps[:, BANK_Y, j * HD:j * HD + HD], pa[:, j, i * P:i * P + P],
                                      v_a[:, v0 + i, (2 * hp + j) * HD:(2 * hp + j + 1) * HD],
                                      start=(i == 0), stop=(i == n - 1))
                    pe.wait_ge(pt_ready[3], s + 1)
                    for j in range(2):
                        acc = ps[:, BANK_Y, (2 + j) * HD:(3 + j) * HD]
                        if whole:
                            pe.matmul(acc, pb[0:CHUNK, j, 0:P],
                                      v_bh[0:CHUNK, t, j * HD:j * HD + HD],
                                      start=True, stop=False)
                        m = pe.matmul(acc, pb[:, j, P:2 * P],
                                      v_b[:, t, j * HD:j * HD + HD],
                                      start=not whole, stop=True)
                    m.then_inc(pv_done, 1)
                    gate_part(hp, range(7, 8)).then_inc(unit_done, 1)

                    if hp == HP - 1:
                        pe.wait_ge(y_ready, s + 1)
                        for br in range(2):
                            for i in range(HP):
                                m = pe.transpose(ps[:, BANK_PT[br], i * P:i * P + P],
                                                 y_rows[:, (br * HP + i) * P:(br * HP + i + 1) * P], ident[:, :])
                            m.then_inc(yt_done, 1)

                pe.wait_ge(proj_read, b * 26 + 26)
                for t in range(TT):
                    for hp in range(HP):
                        step(t, hp)

                pe.wait_ge(scores_read, (b * STEPS + STEPS) * 2)
                for c in range(KT):
                    pe.wait_ge(lo_ready, b * UNITS + U_M + c + 1)
                    if c >= 2:
                        pe.wait_ge(merge_read, b * KT + c - 1)
                    for br in range(2):
                        for i in range(HP):
                            k = br * HP + i
                            if c == 0:
                                pe.wait_ge(yT_lo, b * KT + k + 1)
                            m = three(ps[:, 2 * (c % 2) + br, :], w_tile(c % 2, k), a_cols(k), i == 0, i == HP - 1)
                    m.then_inc(unit_done, 1)

                pe.wait_ge(gate_read, b * STEPS + STEPS)
                for u in range(U_O, UNITS):
                    half, i0 = (u - U_O) // 4, (u - U_O) % 4
                    pe.wait_ge(lo_ready, b * UNITS + u + 1)
                    if u == U_O:
                        pe.wait_ge(m_lo, b * KT + KT)
                    for t in range(TT):
                        for i in range(2):
                            k = 2 * i0 + i
                            m = three(ps[:, 4 + t if half == 0 else t, :], m_tile(k, t), w_row(u % 2, i), k == 0, k == KT - 1)
                    m.then_inc(unit_done, 1)

            pe.wait_ge(ready["ident"], 1)
            body(0, True)
            with pe.Fori(1, NB) as b:
                body(b, False)


_INS = ["x", "g_pre", "w_in", "rel_bias", "sinks", "w_branch_a", "w_branch_b", "w_out", "g_post"]


def kernel(**inputs):
    import numpy as _np
    import concourse.bacc as _bacc
    from concourse import mybir as _mybir
    from concourse.bass_utils import run_bass_kernel_spmd as _run

    nc = _bacc.Bacc("TRN2", target_bir_lowering=False, num_devices=1, dynamic_dma_scratch_size=4096)
    arrays, args = {}, []
    for name in _INS:
        a = _np.ascontiguousarray(inputs[name])
        arrays[f"in_{name}"] = a
        args.append(nc.dram_tensor(f"in_{name}", a.shape, _mybir.dt.from_np(a.dtype), kind="ExternalInput").ap())
    shape = tuple(inputs["x"].shape)
    args.append(nc.dram_tensor("out_x", shape, F32, kind="ExternalOutput").ap())
    build_block(nc, *args)
    r = _run(nc, [arrays], core_ids=[0])
    return r.results[0]["out_x"]
```

```python
from contextlib import ExitStack

import concourse.bass as bass
from concourse import mybir

F32 = mybir.dt.float32
F32R = mybir.dt.float32r
ALU = mybir.AluOpType
ACT = mybir.ActivationFunctionType
AX = mybir.AxisListType

P = 128
D = 1024
KT = D // P
HD = 64
CHUNK = 64
NH = 8
HP = NH // 2
BLK = 512
TT = BLK // P
A_TILES = 5
A_KEYS = A_TILES * P
B_KEYS = 3 * CHUNK
REL = 513
REL_ROW = A_KEYS + P
REL_NEAR = REL_ROW - (A_KEYS - 1 - REL // 2)
EPS = 1e-6
MASKED = -1e30
FAR = 1e33
C_QA, C_KA, C_VA, C_ZA, C_QB, C_KB, C_VB, C_ZB, C_G = 0, 512, 1024, 1536, 2048, 2560, 2688, 2816, 3328

U_VA, U_KB, U_VB, U_KA, U_QA, U_QB, U_ZA, U_ZB, U_G, U_M, U_O, UNITS = 0, 4, 5, 6, 10, 14, 18, 22, 26, 42, 50, 58
T_GROUPS = (C_KA, C_QA, C_QB, C_ZA, C_ZB)
STEPS = TT * HP

BANK_VA = (0, 1, 2, 3)
BANK_KB, BANK_VB = 4, 5
BANK_T = (7, 6)
BANK_H = (4, 5, 6, 7) * 2
BANK_PT = (4, 5)
BANK_Y, BANK_G = 6, 7


def slot_fill(u):
    order = [(U_VA, 0, 1), (U_VA + 2, 1, 1), (U_KB, 0, 1)]
    for u0 in range(U_KA, UNITS, 4):
        n = 2 if U_M <= u0 < U_O else 1
        order += [(u0, 0, n), (u0 + 2, 1, n)]
    count = [0, 0]
    for first, slot, n in order:
        count[slot] += n
        if first <= u < first + 2:
            return slot, count[slot]
    return count


FILLS = slot_fill(UNITS)


def build_block(nc, x, g_pre, w_in, rel_bias, sinks, w_branch_a, w_branch_b, w_out, g_post, out):
    S = x.shape[1]
    NB = S // BLK
    x_v = x.rearrange("a (b t p) d -> a b p t d", p=P, t=TT)[0]
    out_v = out.rearrange("a (b t p) d -> a b p t d", p=P, t=TT)[0]
    w_in_v = w_in[0].rearrange("(k p) c -> p k c", p=P)
    wa_v = w_branch_a[0].rearrange("(k p) c -> p k c", p=P)
    wb_v = w_branch_b[0].rearrange("(k p) c -> p k c", p=P)
    w_out_v = w_out[0].rearrange("(k p) c -> p k c", p=P)
    rel_rows = nc.dram_tensor("rel_rows", (NH, P, REL_ROW), F32, kind="Internal").ap()

    with ExitStack() as ctx:
        def sb(name, shape, dt=F32):
            return ctx.enter_context(nc.sbuf_tensor(name, shape, dt))

        def sem(name):
            return ctx.enter_context(nc.semaphore(name))

        act_hi = sb("act_hi", [P, KT, BLK], F32R)
        act_lo = sb("act_lo", [P, KT, BLK], F32R)
        zx = sb("zx", [P, KT, BLK])
        x_rows = zx[:, :, :].rearrange("p k n -> p (k n)").rearrange("p (t d) -> p t d", t=TT)
        gates_at = -(-nc.sbuf_base // 32) * 32
        gates = sb("gates", [P, 2 * KT, BLK])
        m_parts = nc.alloc_sbuf_tensor_at("m_parts", [P, 2 * KT, BLK], F32R, offset=gates_at)
        q_at = -(-nc.sbuf_base // 32) * 32
        q = sb("q", [P, 2 * HP, BLK])
        y_a = nc.alloc_sbuf_tensor_at("y_a", [P, 2 * HP, BLK], F32R, offset=q_at)
        out_rows = q[:, :, :].rearrange("p k n -> p (k n)").rearrange("p (t d) -> p t d", t=TT)
        k_a = sb("k_a", [P, HP, 2 * BLK])
        v_a = sb("v_a", [P, 2 * TT, NH * HD])
        k_b = sb("k_b", [P, HD + BLK])
        v_b = sb("v_b", [P, TT, 2 * HD])
        v_bh = sb("v_bh", [P, TT + 1, 2 * HD])
        bias_a = sb("bias_a", [P, NH, A_KEYS])
        dist_b = sb("dist_b", [P, B_KEYS])
        w_raw = sb("w_raw", [P, 2, 2048])
        w_hi = sb("w_hi", [P, 2, 1024], F32R)
        w_lo = sb("w_lo", [P, 2, 1024], F32R)
        pa = sb("pa", [P, 2, 2, A_KEYS])
        pb = sb("pb", [P, 2, 2, 2 * P])
        y_rows = sb("y_rows", [P, 2 * NH * HD])
        squares = sb("squares", [P, 1024])
        gpost = sb("gpost", [P, D])
        gpre = sb("gpre", [P, KT])
        ident = sb("ident", [P, P])
        sink = sb("sink", [P, 2, HP])
        nsink = sb("nsink", [P, 2, HP])
        rmax = sb("rmax", [P, 4])
        nmax = sb("nmax", [P, 4])
        rsum = sb("rsum", [P, 2, 4])
        rinv = sb("rinv", [P, 4])
        esink = sb("esink", [P, 2])
        ssx = sb("ssx", [P, TT])
        ssq = sb("ssq", [P, 2, TT])
        mhalf = sb("mhalf", [P, TT])
        var = sb("var", [P, TT])
        r0 = sb("r0", [P, TT])
        r1 = sb("r1", [P, TT])
        rstd = sb("rstd", [P, TT])
        ps = ctx.enter_context(nc.psum_tensor("ps", [P, 8, 512], F32))
        scores = [ps[:, 2 * j:2 * j + 2, :].rearrange("p b n -> p (b n)") for j in range(2)]
        hi_r, lo_r = m_parts[:, 0:KT, :], m_parts[:, KT:2 * KT, :]

        def cols(w, slot):
            return w[:, slot, :].rearrange("p (k c) -> p k c", k=KT)

        def rows(w, slot):
            return w[:, slot, :].rearrange("p (k c) -> p k c", k=2)

        def as_f32(ap):
            return ap.bitcast(F32)

        def res_rows(t):
            return (pa[:, 0, :, :].rearrange("p j n -> p (j n)")[:, 0:D],
                    pa[:, 1, :, :].rearrange("p j n -> p (j n)")[:, 0:D],
                    pb[:, :, :, :].rearrange("p a j n -> p (a j n)"), y_rows[:, :])[t]

        def raw_cols(slot, half):
            return w_raw[:, slot, :].rearrange("p (k c) -> p k c", k=KT)[:, :, half * P:half * P + P]

        def raw_unit(u):
            slot, _ = slot_fill(u)
            half = u % 2
            if u < U_KB or u >= U_O:
                return w_raw[:, slot, half * 1024:half * 1024 + 1024]
            return raw_cols(slot, half)

        def part_unit(w, u):
            if u < U_KB or u >= U_O:
                return w[:, u % 2, :]
            return cols(w, u % 2)

        raw_full = [sem("raw_full0"), sem("raw_full1")]
        hi_ready = sem("hi_ready")
        lo_ready = sem("lo_ready")
        unit_done = sem("unit_done")
        x_full = [sem(f"x_full{t}") for t in range(TT)]
        sq_done = sem("sq_done")
        var_x = sem("var_x")
        pow_done = sem("pow_done")
        newton = sem("newton")
        h_ready = sem("h_ready")
        turned = sem("turned")
        hT_hi = sem("hT_hi")
        hT_lo = sem("hT_lo")
        tanh_done = sem("tanh_done")
        proj_read = sem("proj_read")
        shifted = sem("shifted")
        qk_done = sem("qk_done")
        biased_b = sem("biased_b")
        nmax_a = sem("nmax_a")
        scores_read = sem("scores_read")
        max_b = sem("max_b")
        nmax_b = sem("nmax_b")
        sink_arg = sem("sink_arg")
        exp_a = sem("exp_a")
        exp_b = sem("exp_b")
        exp_sink = sem("exp_sink")
        sum_b = sem("sum_b")
        inv_ready = sem("inv_ready")
        turn = [sem(f"turn{i}") for i in range(4)]
        pt_ready = [sem(f"pt_ready{i}") for i in range(4)]
        pv_done = sem("pv_done")
        y_ready = sem("y_ready")
        yt_done = sem("yt_done")
        yt_read = sem("yt_read")
        gate_read = sem("gate_read")
        yT_hi = sem("yT_hi")
        yT_lo = sem("yT_lo")
        merge_read = sem("merge_read")
        m_sum = sem("m_sum")
        m_hi = sem("m_hi")
        m_lo = sem("m_lo")
        out_sq = sem("out_sq")
        sq_sum = sem("sq_sum")
        var_o = sem("var_o")
        weighed = sem("weighed")
        added = sem("added")
        res_full = sem("res_full")
        stored = sem("stored")
        ready = {n: sem(f"c_{n}") for n in ("dma", "ident0", "ident", "dist0", "dist1", "rel", "relrow", "relst",
                                            "bias", "mask", "nsink", "mhalf")}

        block = ctx.enter_context(nc.Block())

        @block.sync
        def _(sp):
            def pair(slot, srcs, b, before):
                if before is not None:
                    sp.wait_ge(hi_ready, b * UNITS + before)
                    sp.wait_ge(lo_ready, b * UNITS + before)
                for dst, src in srcs(w_raw[:, slot, :]):
                    sp.dma_start(dst, src).then_inc(raw_full[slot], 16)

            def w_cols(c):
                return lambda raw: [(raw.rearrange("p (k c) -> p k c", k=KT), w_in_v[:, :, c])]

            def w_rows(src, k, c):
                return lambda raw: [(raw.rearrange("p (k c) -> p k c", k=4), src[:, k:k + 4, c:c + 512])]

            def w_branches(c):
                def srcs(raw):
                    v = raw.rearrange("p (k c) -> p k c", k=KT)
                    return [(v[:, 0:4, :], wa_v[:, :, c]), (v[:, 4:8, :], wb_v[:, :, c])]
                return srcs

            def store_rows(b):
                for t in range(TT):
                    sp.wait_ge(added, b * TT + t + 1)
                    sp.dma_start(out_v[b][:, t, :], out_rows[:, t, :]).then_inc(stored, 16)

            def body(b, first, last):
                pair(0, w_rows(w_in_v, 0, C_VA), b, None if first else -2)
                pair(1, w_rows(w_in_v, 4, C_VA), b, None if first else 0)
                pair(0, w_cols(slice(C_KB, C_KB + 256)), b, U_VA + 2)
                if not first:
                    store_rows(b - 1)
                for n, c in enumerate(T_GROUPS):
                    u0 = U_KA + 4 * n
                    pair(0, w_cols(slice(c, c + 256)), b, u0 - 2 if n else U_KA)
                    pair(1, w_cols(slice(c + 256, c + 512)), b, u0 if n else U_KB)
                with sp.Fori(0, 4) as i:
                    bb = b * UNITS + i * 4 + U_G
                    for slot in range(2):
                        sp.wait_ge(hi_ready, bb + (2 * slot - 2))
                        sp.wait_ge(lo_ready, bb + (2 * slot - 2))
                        sp.dma_start(w_raw[:, slot, :].rearrange("p (k c) -> p k c", k=KT),
                                     w_in_v[:, :, bass.ds(i * 512 + (C_G + 256 * slot), 256)]).then_inc(raw_full[slot], 16)
                for u0 in range(U_M, U_O, 4):
                    for slot in range(2):
                        c = 128 * (u0 - U_M + 2 * slot)
                        pair(slot, w_branches(slice(c, c + 256)), b, u0 + 2 * slot - 2)
                    if u0 == U_M and not last:
                        sp.wait_ge(yT_hi, b * KT + KT)
                        sp.wait_ge(yT_lo, b * KT + KT)
                        for t in range(TT):
                            sp.dma_start(x_rows[:, t, :], x_v[b + 1][:, t, :]).then_inc(x_full[t], 16)
                for u0 in range(U_O, UNITS, 4):
                    for slot in range(2):
                        if u0 + 2 * slot == UNITS - 2:
                            sp.wait_ge(m_lo, b * KT + KT)
                            sp.wait_ge(m_hi, b * KT + KT)
                            for t in range(TT):
                                sp.dma_start(res_rows(t), x_v[b][:, t, :]).then_inc(res_full, 16)
                        pair(slot, w_rows(w_out_v, 4 * slot, 128 * (u0 - U_O)), b, u0 + 2 * slot - 2)

            for t in range(TT):
                sp.dma_start(x_rows[:, t, :], x_v[0][:, t, :]).then_inc(x_full[t], 16)
            sp.dma_start(pa[0:NH, 0, 0, 0:REL], rel_bias[0]).then_inc(ready["rel"], 16)
            with nc.allow_non_contiguous_dma(reason="1024 words, once"):
                sp.dma_start(gpre[:, :], g_pre[0].rearrange("(k p) -> p k", p=P)).then_inc(ready["dma"], 16)
            sp.dma_start(sink[:, :, :].rearrange("p j i -> p (j i)"), sinks[0:1, :].broadcast_to([P, NH])).then_inc(ready["dma"], 16)
            sp.dma_start(gpost[:, :], g_post[0:1, :].broadcast_to([P, D])).then_inc(ready["dma"], 16)
            body(0, True, False)
            with sp.Fori(1, NB - 1) as b:
                body(b, False, False)
            body(NB - 1, False, True)
            store_rows(NB - 1)
            sp.wait_ge(stored, NB * TT * 16)

        @block.gpsimd
        def _(pool):
            def guess(sem, count):
                pool.wait_ge(sem, count)
                pool.tensor_tensor(r0[:, :], var[:, :], mhalf[:, :], ALU.pow).then_inc(pow_done, 1)

            def body(b, first, last):
                if not last:
                    guess(var_x, b + 2)
                guess(var_o, b + 1)

            pool.memset(mhalf[:, :], -0.5).then_inc(ready["mhalf"], 1)
            pool.memset(ident[:, :], 0.0).then_inc(ready["ident0"], 1)
            pool.wait_ge(ready["ident0"], 1)
            pool.affine_select(out=ident[:, :], in_=ident[:, :], compare_op=ALU.not_equal, fill=1.0, base=0,
                               pattern=[[-1, P]], channel_multiplier=1).then_inc(ready["ident"], 1)
            pool.iota(dist_b[:, :], pattern=[[-1, B_KEYS]], base=CHUNK, channel_multiplier=1,
                      allow_small_or_imprecise_dtypes=True).then_inc(ready["dist0"], 1)
            guess(var_x, 1)
            pool.wait_ge(ready["relrow"], 2)
            pool.dma_start(rel_rows, gates[0:NH, 0:2, :].rearrange("h a n -> h (a n)")[:, 0:REL_ROW]
                           .unsqueeze(1).broadcast_to([NH, P, REL_ROW])).then_inc(ready["relst"], 16)
            pool.wait_ge(ready["relst"], 16)
            pool.dma_start(bias_a[:, :, :], bass.AP(
                tensor=rel_rows.tensor, offset=P - 1,
                ap=[[REL_ROW - 1, P], [P * REL_ROW, NH], [1, A_KEYS]])).then_inc(ready["bias"], 16)
            pool.wait_ge(ready["bias"], 16)
            pool.wait_ge(ready["dist1"], 1)
            for n, (place, value) in enumerate([(bias_a[0:HD, :, A_KEYS - CHUNK:A_KEYS], MASKED),
                                                (bias_a[HD:P, :, 0:CHUNK], MASKED),
                                                (dist_b[0:HD, 2 * CHUNK:B_KEYS], FAR),
                                                (dist_b[HD:P, 0:CHUNK], FAR)]):
                if n:
                    pool.wait_ge(ready["mask"], n)
                pool.memset(place, value).then_inc(ready["mask"], 1)
            pool.wait_ge(ready["mask"], 4)
            body(0, True, False)
            with pool.Fori(1, NB - 1) as b:
                body(b, False, False)
            body(NB - 1, False, True)

        @block.scalar
        def _(act):
            def split_hi(b, u, first, loop=0):
                slot, fill = slot_fill(u)
                act.wait_ge(raw_full[slot], b * (16 * FILLS[slot]) + loop * 16 + fill * 16)
                if not (first and u < 2):
                    act.wait_ge(unit_done, b * UNITS + loop * 4 + (u - 1))
                act.activation(part_unit(w_hi, u), raw_unit(u), ACT.Copy).then_inc(hi_ready, 1)

            def x_square(b, t, outs):
                act.wait_ge(x_full[t], b * 16 + 16)
                if outs is not None:
                    act.wait_ge(out_sq, outs)
                if t:
                    act.wait_ge(sq_done, b * TT + t)
                act.activation(squares[:, :], x_rows[:, t, :], ACT.Square, accum_out=ssx[:, t:t + 1])\
                   .then_inc(sq_done, 1)

            def h_high(b, k):
                for k in range(k, k + HP):
                    act.wait_ge(turned, b * KT + k + 1)
                    act.activation(act_hi[:, k, :], ps[:, BANK_H[k], :], ACT.Copy, scale=gpre[:, k:k + 1])\
                       .then_inc(hT_hi, 1)

            def body(b, first, last):
                def exps(t, hp):
                    s = b * STEPS + t * HP + hp
                    par = hp % 2
                    n = t + 1 if first else A_TILES
                    nb = 2 * CHUNK if first and t == 0 else B_KEYS
                    act.wait_ge(nmax_a, s + 1)
                    for j in range(2):
                        act.activation(pa[:, par, j, 0:n * P], pa[:, par, j, 0:n * P], ACT.Exp, bias=nmax[:, j:j + 1],
                                       accum_out=rsum[:, par, j:j + 1]).then_inc(exp_a, 1)
                    act.wait_ge(nmax_b, s + 1)
                    for j in range(2):
                        act.activation(pb[:, par, j, B_KEYS - nb:B_KEYS], pb[:, par, j, B_KEYS - nb:B_KEYS], ACT.Exp,
                                       bias=nmax[:, 2 + j:3 + j], accum_out=rsum[:, par, 2 + j:3 + j]).then_inc(exp_b, 1)
                    act.wait_ge(sink_arg, s + 1)
                    act.activation(esink[:, :], esink[:, :], ACT.Exp).then_inc(exp_sink, 1)

                def step(i):
                    t, hp = divmod(i - 1, HP)
                    s = b * STEPS + i - 1
                    m = min(t + 1 if first else A_TILES, 4) * P
                    for j in range(2):
                        act.wait_ge(turn[j], s + 1)
                        act.activation(pa[:, hp % 2, j, 0:m], ps[:, BANK_PT[j], 0:m], ACT.Copy).then_inc(pt_ready[j], 1)
                    if i < STEPS:
                        exps(*divmod(i, HP))
                    if i == STEPS:
                        act.wait_ge(yt_read, b * (2 * TT) + 2 * TT - 1)
                        for k in range(HP):
                            act.activation(y_a[:, k, :], zx[:, k, :], ACT.Copy).then_inc(yT_hi, 1)
                    act.wait_ge(unit_done, b * UNITS + (U_G + i))
                    if i == STEPS:
                        act.wait_ge(yt_read, b * (2 * TT) + 2 * TT)
                        for k in range(HP, KT):
                            act.activation(act_hi[:, k, :], zx[:, k, :], ACT.Copy).then_inc(yT_hi, 1)
                        split_hi(b, U_M + 1, first)
                    act.activation(gates[:, i - 1, :], ps[:, BANK_G, :], ACT.Tanh, scale=0.5).then_inc(gate_read, 1)
                    if i < STEPS:
                        split_hi(b, U_G + i + 1, first)

                for u in range(U_G):
                    if U_ZA <= u < U_G:
                        act.wait_ge(unit_done, b * UNITS + u + 1)
                        act.activation(zx[:, u - U_ZA, :], ps[:, BANK_T[u % 2], :], ACT.Tanh, scale=0.5)\
                           .then_inc(tanh_done, 1)
                    split_hi(b, u + 2, first)
                    if u == U_G - 2:
                        exps(0, 0)

                for i in range(1, STEPS + 1):
                    step(i)


                for c in range(KT):
                    split_hi(b, U_M + c + 2, first)
                    act.wait_ge(m_sum, b * KT + c + 1)
                    act.activation(hi_r[:, c, :], pa[:, c % 2, 0, 0:BLK], ACT.Copy).then_inc(m_hi, 1)
                    if 2 <= c < 6 and not last:
                        x_square(b + 1, c - 2, None if first or c > 2 else b * (2 * TT))

                for u in range(U_O, UNITS):
                    if u + 2 < UNITS:
                        split_hi(b, u + 2, first)
                    elif not last:
                        split_hi(b + 1, u + 2 - UNITS, False)
                    if u == U_O and not last:
                        act.wait_ge(merge_read, b * KT + KT)
                        h_high(b + 1, 0)
                    if u == U_O + 1 and not last:
                        h_high(b + 1, HP)
                    if u == U_O + 3:
                        for t in range(TT):
                            square(b, last, t, 0)
                    if u == U_O + 1 and not last:
                        act.activation(k_a[:, :, 0:BLK], k_a[:, :, BLK:2 * BLK], ACT.Copy).then_inc(shifted, 1)
                    if u == U_O + 2 and not last:
                        act.activation(v_a[:, 0:TT, :], v_a[:, TT:2 * TT, :], ACT.Copy).then_inc(shifted, 1)
                        act.activation(k_b[:, 0:HD], k_b[:, BLK:BLK + HD], ACT.Copy).then_inc(shifted, 1)
                        act.activation(v_bh[0:HD, 0, :], v_bh[0:HD, TT, :], ACT.Copy).then_inc(shifted, 1)
                for t in range(TT):
                    square(b, last, t, 1)

            def square(b, last, t, half):
                n = half * TT + t
                act.wait_ge(unit_done, b * UNITS + (U_O + 4 + 4 * half))
                if n >= 2:
                    act.wait_ge(out_sq, b * (2 * TT) + (n - 1))
                else:
                    act.wait_ge(sq_done, b * TT + (TT if last else 2 * TT))
                act.activation(squares[:, 512 * (n % 2):512 * (n % 2) + 512], ps[:, half * TT + t, :], ACT.Square,
                               accum_out=ssq[:, half, t:t + 1]).then_inc(out_sq, 1)

            for t in range(TT):
                x_square(0, t, None)
            split_hi(0, 0, True)
            split_hi(0, 1, True)
            act.wait_ge(ready["dma"], 48)
            h_high(0, 0)
            h_high(0, HP)
            body(0, True, False)
            with act.Fori(1, NB - 1) as b:
                body(b, False, False)
            body(NB - 1, False, True)

        @block.vector
        def _(dve):
            def split_lo(b, u, t=0):
                dve.wait_ge(hi_ready, b * UNITS + t * 4 + (u + 1))
                dve.tensor_tensor(part_unit(w_lo, u), raw_unit(u), as_f32(part_unit(w_hi, u)), ALU.subtract)\
                   .then_inc(lo_ready, 1)

            def refine(n):
                dve.wait_ge(pow_done, n + 1)
                dve.tensor_tensor(r1[:, :], r0[:, :], r0[:, :], ALU.mult).then_inc(newton, 1)
                dve.wait_ge(newton, n * 4 + 1)
                dve.tensor_tensor(r1[:, :], r1[:, :], var[:, :], ALU.mult).then_inc(newton, 1)
                dve.wait_ge(newton, n * 4 + 2)
                dve.tensor_scalar(r1[:, :], r1[:, :], -0.5, 1.5, ALU.mult, ALU.add).then_inc(newton, 1)
                dve.wait_ge(newton, n * 4 + 3)
                dve.tensor_tensor(rstd[:, :], r1[:, :], r0[:, :], ALU.mult).then_inc(newton, 1)
                dve.wait_ge(newton, n * 4 + 4)

            def x_var(b):
                dve.wait_ge(sq_done, b * TT + TT)
                dve.tensor_scalar(var[:, :], ssx[:, :], 1.0 / D, EPS, ALU.mult, ALU.add).then_inc(var_x, 1)

            def x_norm(t):
                dve.tensor_scalar(x_rows[:, t, :], x_rows[:, t, :], rstd[:, t:t + 1], None, ALU.mult)\
                   .then_inc(h_ready, 1)

            def h_low(b, k):
                for k in range(k, k + HP):
                    dve.wait_ge(hT_hi, b * KT + k + 1)
                    dve.scalar_tensor_tensor(out=act_lo[:, k, :], in0=ps[:, BANK_H[k], :], scalar=gpre[:, k:k + 1],
                                             in1=as_f32(act_hi[:, k, :]), op0=ALU.mult, op1=ALU.subtract)\
                       .then_inc(hT_lo, 1)

            def add_rows(b, t):
                if t == 0:
                    dve.wait_ge(weighed, b * (2 * TT) + 2 * TT)
                    dve.wait_ge(res_full, b * (16 * TT) + 16 * TT)
                dve.scalar_tensor_tensor(out=out_rows[:, t, :], in0=out_rows[:, t, :], scalar=rstd[:, t:t + 1],
                                         in1=res_rows(t), op0=ALU.mult, op1=ALU.add).then_inc(added, 1)

            def body(b, first, last):
                def scores_of(t, hp):
                    s = b * STEPS + t * HP + hp
                    par = hp % 2
                    n = t + 1 if first else A_TILES
                    b0 = CHUNK if first and t == 0 else 0
                    dve.wait_ge(qk_done, s + 1)
                    for j in range(2):
                        slope = 2.0 ** (-8.0 / NH * (hp + HP * j + 1))
                        dve.scalar_tensor_tensor(out=pb[:, par, j, b0:B_KEYS], in0=dist_b[:, b0:B_KEYS], scalar=-slope,
                                                 in1=scores[j][:, A_KEYS + b0:A_KEYS + B_KEYS],
                                                 op0=ALU.mult, op1=ALU.add).then_inc(biased_b, 1)
                    for j in range(2):
                        dve.tensor_tensor_reduce(pa[:, par, j, 0:n * P], scores[j][:, 0:n * P],
                                                 bias_a[:, 2 * hp + j, A_KEYS - n * P:A_KEYS], 1.0, -3e38,
                                                 ALU.add, ALU.max, rmax[:, j:j + 1]).then_inc(scores_read, 1)
                    dve.wait_ge(scores_read, s * 2 + 2)
                    dve.tensor_scalar(nmax[:, 0:2], rmax[:, 0:2], -1.0, None, ALU.mult).then_inc(nmax_a, 1)
                    dve.wait_ge(biased_b, s * 2 + 2)
                    dve.tensor_reduce(rmax[:, 2:4], pb[:, par, :, b0:B_KEYS], AX.X, ALU.max).then_inc(max_b, 1)
                    dve.wait_ge(max_b, s + 1)
                    dve.scalar_tensor_tensor(out=nmax[:, 2:4], in0=rmax[:, 2:4], scalar=-1.0, in1=nsink[:, :, hp],
                                             op0=ALU.mult, op1=ALU.min).then_inc(nmax_b, 1)
                    dve.wait_ge(nmax_b, s + 1)
                    dve.tensor_tensor(esink[:, :], sink[:, :, hp], nmax[:, 2:4], ALU.add).then_inc(sink_arg, 1)

                def values_of(t, hp):
                    s = b * STEPS + t * HP + hp
                    par = hp % 2
                    if not first:
                        dve.wait_ge(turn[2], s - STEPS + 1)
                        dve.tensor_copy(pa[:, par, :, 4 * P:5 * P],
                                        ps[:, BANK_PT[0], 0:2 * P].rearrange("p (j n) -> p j n", j=2))\
                           .then_inc(pt_ready[2], 1)
                    dve.wait_ge(turn[3], s + 1)
                    turned_b = ps[:, BANK_PT[1], :].rearrange("p (j n) -> p j n", j=2)
                    if not (first and t == 0):
                        dve.tensor_copy(pb[0:HD, par, :, 0:P], turned_b[0:HD, :, 0:P])
                    dve.tensor_copy(pb[:, par, :, P:2 * P], turned_b[:, :, P:2 * P]).then_inc(pt_ready[3], 1)
                    dve.wait_ge(inv_ready, s + 1)
                    dve.wait_ge(pv_done, s + 1)
                    y_h = y_rows[:, :].rearrange("p (h d) -> p h d", d=HD)
                    acc = ps[:, BANK_Y, 0:4 * HD].rearrange("p (h d) -> p h d", d=HD)
                    dve.tensor_tensor(y_h[:, 2 * hp:2 * hp + 2, :], acc[:, 0:2, :],
                                      rinv[:, 0:2].unsqueeze(2).broadcast_to([P, 2, HD]), ALU.mult)
                    dve.tensor_tensor(y_h[:, NH + hp:NH + hp + HP + 1:HP, :], acc[:, 2:4, :],
                                      rinv[:, 2:4].unsqueeze(2).broadcast_to([P, 2, HD]), ALU.mult).then_inc(y_ready, 1)

                def inverse_of(t, hp):
                    s = b * STEPS + t * HP + hp
                    par = hp % 2
                    dve.wait_ge(exp_sink, s + 1)
                    dve.tensor_tensor(rsum[:, par, 2:4], rsum[:, par, 2:4], esink[:, :], ALU.add).then_inc(sum_b, 1)
                    dve.wait_ge(sum_b, s + 1)
                    dve.reciprocal(rinv[:, :], rsum[:, par, :]).then_inc(inv_ready, 1)

                def gate_y(t):
                    for br in range(2):
                        z_t = zx[:, br * HP:br * HP + HP, t * P:t * P + P]
                        dve.wait_ge(yt_done, b * (2 * TT) + (t * 2 + br + 1))
                        dve.tensor_tensor(z_t, ps[:, BANK_PT[br], :].rearrange("p (k n) -> p k n", k=HP), z_t, ALU.mult)\
                           .then_inc(yt_read, 1)

                for u in range(U_G):
                    if u >= U_KB:
                        dve.wait_ge(unit_done, b * UNITS + u + 1)
                    bank = ps[:, BANK_T[u % 2], :]
                    if u == U_KB:
                        if not first:
                            dve.wait_ge(shifted, b * 4)
                        dve.tensor_copy(k_b[:, HD:HD + BLK], ps[:, BANK_KB, :]).then_inc(proj_read, 1)
                    elif u == U_VB:
                        if not first:
                            dve.wait_ge(shifted, b * 4)
                        dve.tensor_copy(v_bh[0:HD, 1:TT + 1, :].rearrange("p t c -> p (t c)"), ps[HD:P, BANK_VB, :])
                        dve.tensor_copy(v_b[:, :, :].rearrange("p t c -> p (t c)"), ps[:, BANK_VB, :])\
                           .then_inc(proj_read, 1)
                    elif U_KA <= u < U_QA:
                        dve.tensor_copy(k_a[:, u - U_KA, BLK:2 * BLK], bank).then_inc(proj_read, 1)
                    elif U_QA <= u < U_QB:
                        if not first and u == U_QA:
                            dve.wait_ge(stored, b * (16 * TT))
                        dve.tensor_scalar(q[:, u - U_QA, :], bank, HD ** -0.5, None, ALU.mult).then_inc(proj_read, 1)
                    elif U_QB <= u < U_ZA:
                        n = u - U_QB
                        half = n // 2
                        for i in range(2):
                            o = dve.tensor_scalar(q[HD * half:HD * half + HD, HP + (2 * n + i) % HP, :],
                                                  ps[HD * i:HD * i + HD, BANK_T[u % 2], :], HD ** -0.5, None, ALU.mult)
                        o.then_inc(proj_read, 1)
                    elif u >= U_ZA:
                        n = u - U_ZA
                        dve.wait_ge(tanh_done, b * KT + n + 1)
                        dve.scalar_tensor_tensor(out=zx[:, n, :], in0=zx[:, n, :], scalar=1.0, in1=bank,
                                                 op0=ALU.add, op1=ALU.mult).then_inc(proj_read, 1)
                    split_lo(b, u + 2)
                    if u < TT and not first:
                        if u == 0:
                            refine(2 * b)
                        add_rows(b - 1, u)
                    if u == U_G - 2:
                        if first:
                            dve.wait_ge(ready["mask"], 4)
                        scores_of(0, 0)
                    if u == U_VA + 3:
                        dve.wait_ge(unit_done, b * UNITS + u + 1)
                        if not first:
                            dve.wait_ge(shifted, b * 4)
                        for t in range(TT):
                            dve.tensor_copy(v_a[:, TT + t, :], ps[:, BANK_VA[t], :]).then_inc(proj_read, 1)

                for i in range(1, STEPS + 1):
                    t, hp = divmod(i - 1, HP)
                    inverse_of(t, hp)
                    if i < STEPS:
                        scores_of(*divmod(i, HP))
                    values_of(t, hp)
                    if hp == HP - 1:
                        gate_y(t)
                    if i < STEPS:
                        split_lo(b, U_G + i + 1)

                for k in range(KT):
                    dve.wait_ge(yT_hi, b * KT + k + 1)
                    hi, lo = (y_a[:, k, :], y_a[:, HP + k, :]) if k < HP else (act_hi[:, k, :], act_lo[:, k, :])
                    dve.tensor_tensor(lo, zx[:, k, :], as_f32(hi), ALU.subtract).then_inc(yT_lo, 1)
                split_lo(b, U_M + 1)

                b_side = pb[:, 0, :, :].rearrange("p j n -> p (j n)")
                for c in range(KT):
                    m = pa[:, c % 2, 0, 0:BLK]
                    dve.wait_ge(unit_done, b * UNITS + U_M + c + 1)
                    dve.scalar_tensor_tensor(out=m, in0=gates[:, c, :], scalar=1.0, in1=ps[:, 2 * (c % 2), :],
                                             op0=ALU.add, op1=ALU.mult)
                    dve.scalar_tensor_tensor(out=b_side, in0=gates[:, KT + c, :], scalar=1.0,
                                             in1=ps[:, 2 * (c % 2) + 1, :], op0=ALU.add, op1=ALU.mult)\
                       .then_inc(merge_read, 1)
                    split_lo(b, U_M + c + 2)
                    dve.wait_ge(merge_read, b * KT + c + 1)
                    dve.tensor_tensor(m, m, b_side, ALU.add).then_inc(m_sum, 1)
                    dve.wait_ge(m_hi, b * KT + c + 1)
                    dve.tensor_tensor(lo_r[:, c, :], m, as_f32(hi_r[:, c, :]), ALU.subtract).then_inc(m_lo, 1)
                    if c == 5 and not last:
                        x_var(b + 1)
                    if c == 6 and not last:
                        refine(2 * b + 1)
                        x_norm(0)
                    if c == 7 and not last:
                        x_norm(1)

                def weigh(t, half):
                    dve.wait_ge(out_sq, b * (2 * TT) + (half * TT + t + 1))
                    dve.tensor_tensor(out_rows[:, t, half * 512:half * 512 + 512], ps[:, half * TT + t, :],
                                      gpost[:, half * 512:half * 512 + 512], ALU.mult).then_inc(weighed, 1)

                for u in range(U_O, UNITS):
                    if u + 2 < UNITS:
                        split_lo(b, u + 2)
                    elif not last:
                        split_lo(b + 1, u + 2 - UNITS)
                    if u == U_O and not last:
                        x_norm(2)
                        x_norm(3)
                        h_low(b + 1, 0)
                    if u == U_O + 1 and not last:
                        h_low(b + 1, HP)
                    if u == U_O + 3:
                        for t in range(TT):
                            weigh(t, 0)
                for t in range(TT):
                    weigh(t, 1)
                dve.tensor_tensor(ssq[:, 0, :], ssq[:, 0, :], ssq[:, 1, :], ALU.add).then_inc(sq_sum, 1)
                dve.wait_ge(sq_sum, b + 1)
                dve.tensor_scalar(var[:, :], ssq[:, 0, :], 1.0 / D, 16 * EPS, ALU.mult, ALU.add).then_inc(var_o, 1)
                if last:
                    refine(2 * b + 1)
                    for t in range(TT):
                        add_rows(b, t)

            x_var(0)
            refine(0)
            for t in range(TT):
                x_norm(t)
            split_lo(0, 0)
            split_lo(0, 1)
            dve.wait_ge(ready["dma"], 48)
            h_low(0, 0)
            h_low(0, HP)
            dve.tensor_scalar(nsink[:, :, :], sink[:, :, :], -1.0, None, ALU.mult).then_inc(ready["nsink"], 1)
            far = REL_ROW - REL_NEAR
            rel_row = gates[0:NH, 0:2, :].rearrange("p a n -> p (a n)")
            dve.wait_ge(ready["rel"], 16)
            dve.tensor_copy(rel_row[:, 0:far], pa[0:NH, 0, 0, REL - 1:REL].broadcast_to([NH, far])).then_inc(ready["relrow"], 1)
            dve.tensor_copy(rel_row[:, far:REL_ROW], pa[0:NH, 0, 0, REL - REL_NEAR:REL][:, ::-1]).then_inc(ready["relrow"], 1)
            dve.wait_ge(ready["dist0"], 1)
            dve.scalar_tensor_tensor(out=dist_b[:, :], in0=dist_b[:, :], scalar=-1.0, in1=dist_b[:, :],
                                     op0=ALU.mult, op1=ALU.max).then_inc(ready["dist1"], 1)
            body(0, True, False)
            with dve.Fori(1, NB - 1) as b:
                body(b, False, False)
            body(NB - 1, False, True)

        @block.tensor
        def _(pe):
            def three(out_ap, lhs, rhs, start, stop):
                (lh, ll), (rh, rl) = lhs, rhs
                pe.matmul(out_ap, lh, rh, start=start, stop=False)
                pe.matmul(out_ap, lh, rl, start=False, stop=False)
                return pe.matmul(out_ap, ll, rh, start=False, stop=stop)

            def w_tile(slot, k):
                return cols(w_hi, slot)[:, k, :], cols(w_lo, slot)[:, k, :]

            def w_row(slot, k):
                return rows(w_hi, slot)[:, k, :], rows(w_lo, slot)[:, k, :]

            def a_cols(k):
                return act_hi[:, k, :], act_lo[:, k, :]

            def y_cols(k):
                if k < HP:
                    return y_a[:, k, :], y_a[:, HP + k, :]
                return a_cols(k)

            def a_tile(k, t):
                return act_hi[:, k, t * P:t * P + P], act_lo[:, k, t * P:t * P + P]

            def m_tile(k, t):
                return hi_r[:, k, t * P:t * P + P], lo_r[:, k, t * P:t * P + P]

            def turn_h(b, k):
                pe.wait_ge(h_ready, b * TT + TT)
                if k:
                    pe.wait_ge(hT_lo, b * KT + k)
                for k in range(k, k + HP):
                    for t in range(TT):
                        m = pe.transpose(ps[:, BANK_H[k], t * P:t * P + P], x_rows[:, t, k * P:k * P + P], ident[:, :])
                    m.then_inc(turned, 1)

            def body(b, first, last):
                if not first:
                    pe.wait_ge(weighed, b * (2 * TT) - TT)
                for u in range(U_VA, U_KB):
                    pe.wait_ge(lo_ready, b * UNITS + u + 1)
                    if first:
                        pe.wait_ge(hT_lo, 2 * u + 2)
                    for t in range(TT):
                        for i in range(2):
                            k = 2 * u + i
                            m = three(ps[:, BANK_VA[t], :], a_tile(k, t), w_row(u % 2, i), k == 0, k == KT - 1)
                    m.then_inc(unit_done, 1)
                pe.wait_ge(lo_ready, b * UNITS + U_KB + 1)
                if not first:
                    pe.wait_ge(weighed, b * (2 * TT))
                for k in range(KT):
                    m = three(ps[:, BANK_KB, :], w_tile(U_KB % 2, k), a_cols(k), k == 0, k == KT - 1)
                m.then_inc(unit_done, 1)
                pe.wait_ge(lo_ready, b * UNITS + U_VB + 1)
                for t in range(TT):
                    for k in range(KT):
                        m = three(ps[:, BANK_VB, t * P:t * P + P], a_tile(k, t), w_tile(U_VB % 2, k), k == 0, k == KT - 1)
                m.then_inc(unit_done, 1)

                def column_unit(u, j):
                    pe.wait_ge(lo_ready, u + 1)
                    for k in range(KT):
                        m = three(ps[:, BANK_T[j], :], w_tile(j, k), a_cols(k), k == 0, k == KT - 1)
                    m.then_inc(unit_done, 1)

                with pe.Fori(0, (U_G - U_KA) // 2 - 1) as i:
                    for j in range(2):
                        pe.wait_ge(proj_read, b * 26 + i * 2 + (U_KA + j - 1))
                        column_unit(b * UNITS + i * 2 + (U_KA + j), j)

                def gate_part(hp, ks):
                    for k in ks:
                        m = three(ps[:, BANK_G, :], w_tile(hp % 2, k), a_cols(k), k == 0, k == KT - 1)
                    return m

                def scores_of(t, hp):
                    s = b * STEPS + t * HP + hp
                    n = t + 1 if first else A_TILES
                    k0 = (TT + t - (n - 1)) * P
                    if (t, hp) != (0, 0):
                        pe.wait_ge(scores_read, s * 2)
                    for j in range(2):
                        rows_j = slice(HD * j, HD * j + HD)
                        q_a, q_b = q[rows_j, hp, t * P:t * P + P], q[rows_j, HP + hp, t * P:t * P + P]
                        m1 = min(n, 4) * P
                        pe.matmul(scores[j][:, 0:m1], q_a, k_a[rows_j, hp, k0:k0 + m1], start=True, stop=True)
                        if n == A_TILES:
                            pe.matmul(scores[j][:, 4 * P:5 * P], q_a, k_a[rows_j, hp, k0 + 4 * P:k0 + 5 * P],
                                      start=True, stop=True)
                        b0 = CHUNK if first and t == 0 else 0
                        m = pe.matmul(scores[j][:, A_KEYS + b0:A_KEYS + B_KEYS], q_b,
                                      k_b[rows_j, t * P + b0:t * P + B_KEYS], start=True, stop=True)
                    m.then_inc(qk_done, 1)

                def step(i):
                    t, hp = divmod(i - 1, HP)
                    s = b * STEPS + i - 1
                    par = hp % 2
                    n = t + 1 if first else A_TILES
                    whole = not (first and t == 0)
                    ks = (2, 4, 6, 8, 8) if i < STEPS else (1, 3, 4, 5, 8)
                    if i < STEPS:
                        scores_of(*divmod(i, HP))
                    pe.wait_ge(lo_ready, b * UNITS + (U_G + i))
                    if i == 1:
                        pe.wait_ge(proj_read, b * 26 + 26)
                    else:
                        pe.wait_ge(gate_read, s)
                    gate_part(hp, range(0, ks[0]))
                    for j in range(2):
                        pe.wait_ge(exp_a, s * 2 + (j + 1))
                        if hp == 0 and not (first and t == 0):
                            pe.wait_ge(yt_read, b * (2 * TT) + (t * 2 - (1 - j)))
                        for x in range(min(n, 4)):
                            m = pe.transpose(ps[:, BANK_PT[j], x * P:x * P + P], pa[:, par, j, x * P:x * P + P], ident[:, :])
                        m.then_inc(turn[j], 1)
                    gate_part(hp, range(ks[0], ks[1]))
                    pe.wait_ge(pt_ready[0], s + 1)
                    if n == A_TILES:
                        for j in range(2):
                            m = pe.transpose(ps[:, BANK_PT[0], j * P:j * P + P], pa[:, par, j, 4 * P:5 * P], ident[:, :])
                        m.then_inc(turn[2], 1)
                    pe.wait_ge(pt_ready[1], s + 1)
                    pe.wait_ge(exp_b, s * 2 + 2)
                    for j in range(2):
                        m = pe.transpose(ps[:, BANK_PT[1], (2 * j + 1) * P:(2 * j + 2) * P], pb[:, par, j, CHUNK:B_KEYS],
                                         ident[:, :])
                        if whole:
                            m = pe.transpose(ps[0:CHUNK, BANK_PT[1], 2 * j * P:2 * j * P + P], pb[:, par, j, 0:CHUNK],
                                             ident[:, :])
                    m.then_inc(turn[3], 1)
                    gate_part(hp, range(ks[1], ks[2]))

                    if i > 1:
                        pe.wait_ge(y_ready, s)
                    v0 = TT + t - (n - 1)
                    if n == A_TILES:
                        pe.wait_ge(pt_ready[2], s - STEPS + 1)
                    for j in range(2):
                        for x in range(n):
                            pe.matmul(ps[:, BANK_Y, j * HD:j * HD + HD], pa[:, par, j, x * P:x * P + P],
                                      v_a[:, v0 + x, (2 * hp + j) * HD:(2 * hp + j + 1) * HD],
                                      start=(x == 0), stop=(x == n - 1))
                    pe.wait_ge(pt_ready[3], s + 1)
                    for j in range(2):
                        acc = ps[:, BANK_Y, (2 + j) * HD:(3 + j) * HD]
                        if whole:
                            pe.matmul(acc, pb[0:CHUNK, par, j, 0:P], v_bh[0:CHUNK, t, j * HD:j * HD + HD],
                                      start=True, stop=False)
                        m = pe.matmul(acc, pb[:, par, j, P:2 * P], v_b[:, t, j * HD:j * HD + HD],
                                      start=not whole, stop=True)
                    m.then_inc(pv_done, 1)
                    m = gate_part(hp, range(ks[2], ks[3]))
                    if i < STEPS:
                        m.then_inc(unit_done, 1)

                    if hp == HP - 1:
                        pe.wait_ge(y_ready, s + 1)
                        for br in range(2):
                            for x in range(HP):
                                m = pe.transpose(ps[:, BANK_PT[br], x * P:x * P + P],
                                                 y_rows[:, (br * HP + x) * P:(br * HP + x + 1) * P], ident[:, :])
                            m.then_inc(yt_done, 1)
                    if i == STEPS:
                        gate_part(hp, range(ks[3], ks[4])).then_inc(unit_done, 1)

                pe.wait_ge(proj_read, b * 26 + (U_G - 3))
                column_unit(b * UNITS + (U_G - 2), 0)
                scores_of(0, 0)
                pe.wait_ge(proj_read, b * 26 + (U_G - 2))
                column_unit(b * UNITS + (U_G - 1), 1)
                for i in range(1, STEPS + 1):
                    step(i)

                pe.wait_ge(scores_read, (b * STEPS + STEPS) * 2)
                for c in range(KT):
                    pe.wait_ge(lo_ready, b * UNITS + U_M + c + 1)
                    if c >= 2:
                        pe.wait_ge(merge_read, b * KT + c - 1)
                    for br in range(2):
                        for i in range(HP):
                            k = br * HP + i
                            if c == 0:
                                pe.wait_ge(yT_lo, b * KT + k + 1)
                            m = three(ps[:, 2 * (c % 2) + br, :], w_tile(c % 2, k), y_cols(k), i == 0, i == HP - 1)
                    m.then_inc(unit_done, 1)

                for u in range(U_O, UNITS):
                    half, i0 = (u - U_O) // 4, (u - U_O) % 4
                    pe.wait_ge(lo_ready, b * UNITS + u + 1)
                    if half == 0:
                        pe.wait_ge(m_lo, b * KT + 2 * i0 + 2)
                    if u == U_O + 4 and not last:
                        pe.wait_ge(hT_lo, b * KT + 2 * KT)
                    for t in range(TT):
                        if u == U_O and t % 2 == 0:
                            pe.wait_ge(merge_read, b * KT + KT - 1 + t // 2)
                        for i in range(2):
                            k = 2 * i0 + i
                            m = three(ps[:, half * TT + t, :], m_tile(k, t), w_row(u % 2, i), k == 0, k == KT - 1)
                    m.then_inc(unit_done, 1)
                    if u == U_O + 1 and not last:
                        pe.wait_ge(gate_read, b * STEPS + STEPS)
                        turn_h(b + 1, 0)
                    if u == U_O + 2 and not last:
                        turn_h(b + 1, HP)

            pe.wait_ge(ready["ident"], 1)
            turn_h(0, 0)
            turn_h(0, HP)
            body(0, True, False)
            with pe.Fori(1, NB - 1) as b:
                body(b, False, False)
            body(NB - 1, False, True)


_INS = ["x", "g_pre", "w_in", "rel_bias", "sinks", "w_branch_a", "w_branch_b", "w_out", "g_post"]


def kernel(**inputs):
    import numpy as _np
    import concourse.bacc as _bacc
    from concourse import mybir as _mybir
    from concourse.bass_utils import run_bass_kernel_spmd as _run

    nc = _bacc.Bacc("TRN2", target_bir_lowering=False, num_devices=1, dynamic_dma_scratch_size=4096)
    arrays, args = {}, []
    for name in _INS:
        a = _np.ascontiguousarray(inputs[name])
        arrays[f"in_{name}"] = a
        args.append(nc.dram_tensor(f"in_{name}", a.shape, _mybir.dt.from_np(a.dtype), kind="ExternalInput").ap())
    shape = tuple(inputs["x"].shape)
    args.append(nc.dram_tensor("out_x", shape, F32, kind="ExternalOutput").ap())
    build_block(nc, *args)
    r = _run(nc, [arrays], core_ids=[0])
    return r.results[0]["out_x"]
```

```python
from contextlib import ExitStack

import concourse.bass as bass
from concourse import mybir

F32 = mybir.dt.float32
F32R = mybir.dt.float32r
BF16 = mybir.dt.bfloat16
ALU = mybir.AluOpType
ACT = mybir.ActivationFunctionType
AX = mybir.AxisListType

P = 128
D = 1024
KT = D // P
HD = 64
CHUNK = 64
NH = 8
HP = NH // 2
BLK = 512
TT = BLK // P
A_TILES = 5
A_KEYS = A_TILES * P
B_KEYS = 3 * CHUNK
REL = 513
REL_ROW = A_KEYS + P
REL_NEAR = REL_ROW - (A_KEYS - 1 - REL // 2)
EPS = 1e-6
MASKED = -1e30
FAR = 1e33
C_QA, C_KA, C_VA, C_ZA, C_QB, C_KB, C_VB, C_ZB, C_G = 0, 512, 1024, 1536, 2048, 2560, 2688, 2816, 3328

U_VA, U_VB, U_KB, U_KA, U_QA, U_QB, U_ZA, U_ZB, U_G, U_M, U_O, UNITS = 0, 4, 5, 6, 10, 14, 18, 22, 26, 42, 50, 58
T_GROUPS = (C_KA, C_QA, C_QB, C_ZA, C_ZB)
STEPS = TT * HP
ALL, PAIRS = slice(0, TT), (slice(0, 2), slice(2, TT))

BANK_VA, BANK_KB, BANK_VB = (0, 1, 2, 3), 4, 5
BANK_VA0, BANK_KB0, BANK_VB0 = (4, 5, 6, 7), 0, 1
BANK_T = (7, 6)
BANK_H = (4, 5, 6, 7) * 2
BANK_H0 = (4, 5, 6, 7, 0, 1, 2, 3)
BANK_PT = (4, 5)
BANK_Y, BANK_G = 6, 7


def slot_fill(u):
    order = [(U_VA, 0, 1), (U_VA + 2, 1, 1), (U_VB, 0, 1)]
    for u0 in range(U_KA, UNITS, 4):
        n = 3 if U_M <= u0 < U_O else 2 if U_QB <= u0 < U_ZA or U_ZB <= u0 < U_G else 1
        order += [(u0, 0, n), (u0 + 2, 1, n)]
    count = [0, 0]
    for first, slot, n in order:
        count[slot] += n
        if first <= u < first + 2:
            return slot, count[slot]
    return count


FILLS = slot_fill(UNITS)


def build_block(nc, x, g_pre, w_in, rel_bias, sinks, w_branch_a, w_branch_b, w_out, g_post, out):
    S = x.shape[1]
    NB = S // BLK
    x_v = x.rearrange("a (b t p) d -> a b p t d", p=P, t=TT)[0]
    out_v = out.rearrange("a (b t p) d -> a b p t d", p=P, t=TT)[0]
    w_in_v = w_in[0].rearrange("(k p) c -> p k c", p=P)
    wa_v = w_branch_a[0].rearrange("(k p) c -> p k c", p=P)
    wb_v = w_branch_b[0].rearrange("(j k p) c -> j p k c", j=2, p=HD)
    w_out_v = w_out[0].rearrange("(k p) c -> p k c", p=P)
    rel_rows = nc.dram_tensor("rel_rows", (NH, P, REL_ROW), F32, kind="Internal").ap()

    with ExitStack() as ctx:
        def sb(name, shape, dt=F32):
            return ctx.enter_context(nc.sbuf_tensor(name, shape, dt))

        def sem(name):
            return ctx.enter_context(nc.semaphore(name))

        act_hi = sb("act_hi", [P, KT, BLK], F32R)
        act_lo = sb("act_lo", [P, KT, BLK], F32R)
        zx = sb("zx", [P, KT, BLK])
        x_rows = zx[:, :, :].rearrange("p k n -> p (k n)").rearrange("p (t d) -> p t d", t=TT)
        gates_at = -(-nc.sbuf_base // 32) * 32
        gates = sb("gates", [P, 2 * KT, BLK])
        m_parts = nc.alloc_sbuf_tensor_at("m_parts", [P, 2 * KT, BLK], F32R, offset=gates_at)
        q_parts = m_parts[:, 2 * KT - 2:2 * KT, :].rearrange("p a (x n) -> p (a x) n", n=P)\
                                                  .rearrange("p (l j b) n -> p l j b n", l=2, j=2)
        q_at = -(-nc.sbuf_base // 32) * 32
        q = sb("q", [P, 2 * HP, BLK])
        y_a = nc.alloc_sbuf_tensor_at("y_a", [P, 2 * HP, BLK], F32R, offset=q_at)
        out_rows = q[:, :, :].rearrange("p k n -> p (k n)").rearrange("p (t d) -> p t d", t=TT)
        k_a = sb("k_a", [P, NH, 2 * BLK], F32R)
        v_a = sb("v_a", [P, 2 * TT, NH * HD])
        k_b = sb("k_b", [P, 2, HD + BLK], F32R)
        v_b = sb("v_b", [P, TT, 2 * HD])
        v_bh = sb("v_bh", [P, TT, 2 * HD])
        bias_a = sb("bias_a", [P, NH, A_KEYS])
        dist_b = sb("dist_b", [P, B_KEYS], BF16)
        w_raw = sb("w_raw", [P, 2, 2048])
        w_hi = sb("w_hi", [P, 2, 1024], F32R)
        w_lo = sb("w_lo", [P, 2, 1024], F32R)
        pa = sb("pa", [P, 2, 2, A_KEYS])
        pb = sb("pb", [P, 2, 2, B_KEYS])
        squares = pa[:, :, 1, 0:BLK]
        gpost = sb("gpost", [P, D])
        gpre = sb("gpre", [P, KT])
        ident = sb("ident", [P, P])
        sink = sb("sink", [P, 2, HP])
        nsink = sb("nsink", [P, 2, HP])
        rmax = sb("rmax", [P, 4])
        nmax = sb("nmax", [P, 4])
        rsum = sb("rsum", [P, 2, 4])
        rinv = sb("rinv", [P, 4])
        esink = sb("esink", [P, 2])
        ssx = sb("ssx", [P, TT])
        ssq = sb("ssq", [P, 2, TT])
        mhalf = sb("mhalf", [P, TT])
        var = sb("var", [P, TT])
        r0 = sb("r0", [P, TT])
        r1 = sb("r1", [P, TT])
        rstd = sb("rstd", [P, TT])
        ps = ctx.enter_context(nc.psum_tensor("ps", [P, 8, 512], F32))
        scores = [ps[:, 2 * j:2 * j + 2, :].rearrange("p b n -> p (b n)") for j in range(2)]
        hi_r, lo_r = m_parts[:, 0:KT, :], m_parts[:, KT:2 * KT, :]

        def cols(w, slot):
            return w[:, slot, :].rearrange("p (k c) -> p k c", k=KT)

        def rows(w, slot):
            return w[:, slot, :].rearrange("p (k c) -> p k c", k=2)

        def as_f32(ap):
            return ap.bitcast(F32)

        def b_thirds(par):
            return pb[:, par, :, :].rearrange("p j n -> p (j n)").rearrange("p (a n) -> p a n", n=P)

        def raw_cols(slot, half):
            return w_raw[:, slot, :].rearrange("p (k c) -> p k c", k=KT)[:, :, half * P:half * P + P]

        def of_heads(u):
            return U_QB <= u < U_ZA or U_ZB <= u < U_G

        def raw_unit(u):
            slot, _ = slot_fill(u)
            half = 1 - u % 2 if U_VB <= u < U_KA + 2 else u % 2
            if u < U_VB or u >= U_O:
                return w_raw[:, slot, half * 1024:half * 1024 + 1024]
            if of_heads(u):
                return w_raw[:, slot, :].rearrange("p (k j i d) -> p k j i d", j=2, i=2, d=HD)[:, :, :, half, :]
            return raw_cols(slot, half)

        def part_unit(w, u):
            if u < U_VB or u >= U_O:
                return w[:, u % 2, :]
            if of_heads(u):
                return w[:, u % 2, :].rearrange("p (k j d) -> p k j d", j=2, d=HD)
            return cols(w, u % 2)

        raw_full = [sem("raw_full0"), sem("raw_full1")]
        hi_ready = sem("hi_ready")
        lo_ready = sem("lo_ready")
        unit_done = sem("unit_done")
        ka_full = sem("ka_full")
        x_full = [sem(f"x_full{t}") for t in range(TT)]
        sq_done = sem("sq_done")
        var_x = sem("var_x")
        pow_done = sem("pow_done")
        newton = sem("newton")
        h_ready = sem("h_ready")
        turned = sem("turned")
        hT_hi = sem("hT_hi")
        hT_lo = sem("hT_lo")
        tanh_done = sem("tanh_done")
        proj_read = sem("proj_read")
        shifted = sem("shifted")
        qk_done = sem("qk_done")
        v_staged = sem("v_staged")
        v_turned = sem("v_turned")
        k_hi = sem("k_hi")
        q_hi = sem("q_hi")
        q_lo = sem("q_lo")
        biased_b = sem("biased_b")
        nmax_a = sem("nmax_a")
        scores_read = sem("scores_read")
        max_b = sem("max_b")
        nmax_b = sem("nmax_b")
        sink_arg = sem("sink_arg")
        exp_a = sem("exp_a")
        exp_b = sem("exp_b")
        exp_sink = sem("exp_sink")
        sum_b = sem("sum_b")
        inv_ready = sem("inv_ready")
        turn = [sem(f"turn{i}") for i in range(4)]
        pt_ready = [sem(f"pt_ready{i}") for i in range(4)]
        pv_done = sem("pv_done")
        y_ready = sem("y_ready")
        yt_done = sem("yt_done")
        yt_read = sem("yt_read")
        gate_read = sem("gate_read")
        yT_hi = sem("yT_hi")
        yT_lo = sem("yT_lo")
        merge_read = sem("merge_read")
        m_sum = sem("m_sum")
        m_hi = sem("m_hi")
        m_lo = sem("m_lo")
        row_done = sem("row_done")
        out_sq = sem("out_sq")
        sq_sum = sem("sq_sum")
        var_o = sem("var_o")
        weighed = sem("weighed")
        added = sem("added")
        res_full = sem("res_full")
        stored = sem("stored")
        ready = {n: sem(f"c_{n}") for n in ("dma", "ident0", "ident", "dist0", "dist1", "rel", "relrow", "relst",
                                            "bias", "mask", "nsink", "mhalf", "v_bh")}

        block = ctx.enter_context(nc.Block())

        @block.sync
        def _(sp):
            def pair(slot, srcs, b, before):
                if before is not None:
                    sp.wait_ge(hi_ready, b * UNITS + before)
                    sp.wait_ge(lo_ready, b * UNITS + before)
                for dst, src in srcs(w_raw[:, slot, :]):
                    sp.dma_start(dst, src).then_inc(raw_full[slot], 16)

            def w_cols(c):
                return lambda raw: [(raw.rearrange("p (k c) -> p k c", k=KT), w_in_v[:, :, c])]

            def w_heads(c, h):
                def srcs(raw):
                    v = raw.rearrange("p (k j n) -> p k j n", k=KT, j=2)
                    return [(v[:, :, j, :], w_in_v[:, :, c + (HP * j + h) * HD:c + (HP * j + h + 2) * HD])
                            for j in range(2)]
                return srcs

            def w_rows(src, k, c):
                return lambda raw: [(raw.rearrange("p (k c) -> p k c", k=4), src[:, k:k + 4, c:c + 512])]

            def w_branches(c):
                def srcs(raw):
                    v = raw.rearrange("p (k c) -> p k c", k=KT)
                    return [(v[:, 0:4, :], wa_v[:, :, c])] + \
                           [(v[HD * j:HD * j + HD, 4:8, :], wb_v[j][:, :, c]) for j in range(2)]
                return srcs

            def store_rows(b):
                for t in range(TT):
                    sp.wait_ge(added, b * TT + t + 1)
                    sp.dma_start(out_v[b][:, t, :], out_rows[:, t, :]).then_inc(stored, 16)

            def body(b, first, last):
                pair(0, w_rows(w_in_v, 0, C_VA), b, None if first else -2)
                pair(1, w_rows(w_in_v, 4, C_VA), b, None if first else 0)
                pair(0, w_cols(slice(C_KB, C_KB + 256)), b, U_VA + 2)
                sp.wait_ge(hi_ready, b * UNITS + U_VB + 1)
                sp.wait_ge(lo_ready, b * UNITS + U_VB + 1)
                sp.dma_start(raw_cols(0, 1), w_in_v[:, :, C_KA:C_KA + P]).then_inc(ka_full, 16)
                if first:
                    sp.wait_ge(ready["relrow"], 2)
                    sp.dma_start(rel_rows, gates[0:NH, 0:2, :].rearrange("h a n -> h (a n)")[:, 0:REL_ROW]
                                 .unsqueeze(1).broadcast_to([NH, P, REL_ROW])).then_inc(ready["relst"], 16)
                else:
                    store_rows(b - 1)
                sp.wait_ge(hi_ready, b * UNITS + U_KB + 1)
                sp.wait_ge(lo_ready, b * UNITS + U_KB + 1)
                sp.dma_start(raw_cols(0, 0), w_in_v[:, :, C_KA + P:C_KA + 2 * P]).then_inc(raw_full[0], 16)
                for n, c in enumerate(T_GROUPS):
                    if first and n == 1:
                        sp.wait_ge(ready["relst"], 16)
                        sp.dma_start(bias_a[:, :, :], bass.AP(
                            tensor=rel_rows.tensor, offset=P - 1,
                            ap=[[REL_ROW - 1, P], [P * REL_ROW, NH], [1, A_KEYS]])).then_inc(ready["bias"], 16)
                    u0 = U_KA + 4 * n
                    halves = [w_heads(c, 0), w_heads(c, 2)] if c in (C_QB, C_ZB) else \
                             [w_cols(slice(c, c + 256)), w_cols(slice(c + 256, c + 512))]
                    if n:
                        pair(0, halves[0], b, u0 - 2)
                    pair(1, halves[1], b, u0 if n else U_VB)
                with sp.Fori(0, 4) as i:
                    bb = b * UNITS + i * 4 + U_G
                    for slot in range(2):
                        sp.wait_ge(hi_ready, bb + (2 * slot - 2))
                        sp.wait_ge(lo_ready, bb + (2 * slot - 2))
                        sp.dma_start(w_raw[:, slot, :].rearrange("p (k c) -> p k c", k=KT),
                                     w_in_v[:, :, bass.ds(i * 512 + (C_G + 256 * slot), 256)]).then_inc(raw_full[slot], 16)
                for u0 in range(U_M, U_O, 4):
                    for slot in range(2):
                        c = 128 * (u0 - U_M + 2 * slot)
                        pair(slot, w_branches(slice(c, c + 256)), b, u0 + 2 * slot - 2)
                    if u0 == U_M and not last:
                        sp.wait_ge(yT_hi, b * KT + KT)
                        sp.wait_ge(yT_lo, b * KT + KT)
                        for t in range(TT):
                            sp.dma_start(x_rows[:, t, :], x_v[b + 1][:, t, :]).then_inc(x_full[t], 16)
                for u0 in range(U_O, UNITS, 4):
                    for slot in range(2):
                        if u0 + 2 * slot == UNITS - 2:
                            if last:
                                sp.wait_ge(yT_hi, b * KT + KT)
                                sp.wait_ge(yT_lo, b * KT + KT)
                            else:
                                sp.wait_ge(turned, b * KT + 2 * KT)
                            for t in range(TT):
                                sp.dma_start(x_rows[:, t, :], x_v[b][:, t, :]).then_inc(res_full, 16)
                        pair(slot, w_rows(w_out_v, 4 * slot, 128 * (u0 - U_O)), b, u0 + 2 * slot - 2)

            for t in range(TT):
                sp.dma_start(x_rows[:, t, :], x_v[0][:, t, :]).then_inc(x_full[t], 16)
            sp.dma_start(pa[0:NH, 0, 0, 0:REL], rel_bias[0]).then_inc(ready["rel"], 16)
            with nc.allow_non_contiguous_dma(reason="1024 words, once"):
                sp.dma_start(gpre[:, :], g_pre[0].rearrange("(k p) -> p k", p=P)).then_inc(ready["dma"], 16)
            sp.dma_start(sink[:, :, :].rearrange("p j i -> p (j i)"), sinks[0:1, :].broadcast_to([P, NH])).then_inc(ready["dma"], 16)
            sp.dma_start(gpost[:, :], g_post[0:1, :].broadcast_to([P, D])).then_inc(ready["dma"], 16)
            body(0, True, False)
            with sp.Fori(1, NB - 1) as b:
                body(b, False, False)
            body(NB - 1, False, True)
            store_rows(NB - 1)
            sp.wait_ge(stored, NB * TT * 16)

        @block.gpsimd
        def _(pool):
            def guess(sem, count, ts=ALL):
                pool.wait_ge(sem, count)
                pool.tensor_tensor(r0[:, ts], var[:, ts], mhalf[:, ts], ALU.pow).then_inc(pow_done, 1)

            def body(b, first, last):
                if not last:
                    guess(var_x, b + 3)
                    guess(var_o, b + 1)
                else:
                    for g, ts in enumerate(PAIRS):
                        guess(var_o, b + 1 + g, ts)

            pool.memset(mhalf[:, :], -0.5).then_inc(ready["mhalf"], 1)
            pool.memset(ident[:, :], 0.0).then_inc(ready["ident0"], 1)
            pool.wait_ge(ready["ident0"], 1)
            pool.affine_select(out=ident[:, :], in_=ident[:, :], compare_op=ALU.not_equal, fill=1.0, base=0,
                               pattern=[[-1, P]], channel_multiplier=1).then_inc(ready["ident"], 1)
            pool.iota(dist_b[:, :], pattern=[[-1, B_KEYS]], base=CHUNK, channel_multiplier=1,
                      allow_small_or_imprecise_dtypes=True).then_inc(ready["dist0"], 1)
            pool.wait_ge(ready["mhalf"], 1)
            for g, ts in enumerate(PAIRS):
                guess(var_x, 1 + g, ts)
            pool.memset(v_bh[:, :, :], 0.0).then_inc(ready["v_bh"], 1)
            pool.wait_ge(ready["bias"], 16)
            pool.wait_ge(ready["dist1"], 1)
            for n, (place, value) in enumerate([(bias_a[0:HD, :, A_KEYS - CHUNK:A_KEYS], MASKED),
                                                (bias_a[HD:P, :, 0:CHUNK], MASKED),
                                                (dist_b[0:HD, 2 * CHUNK:B_KEYS], FAR),
                                                (dist_b[HD:P, 0:CHUNK], FAR)]):
                if n:
                    pool.wait_ge(ready["mask"], n)
                pool.memset(place, value).then_inc(ready["mask"], 1)
            pool.wait_ge(ready["mask"], 4)
            body(0, True, False)
            with pool.Fori(1, NB - 1) as b:
                body(b, False, False)
            body(NB - 1, False, True)

        @block.scalar
        def _(act):
            def split_hi(b, u, first):
                slot, fill = slot_fill(u)
                if u == U_KA:
                    act.wait_ge(ka_full, b * 16 + 16)
                else:
                    act.wait_ge(raw_full[slot], b * (16 * FILLS[slot]) + fill * 16)
                if not (first and u < 2):
                    act.wait_ge(unit_done, b * UNITS + (u - 1))
                act.activation(part_unit(w_hi, u), raw_unit(u), ACT.Copy).then_inc(hi_ready, 1)

            def x_square(b, t, outs):
                act.wait_ge(x_full[t], b * 16 + 16)
                if outs is not None:
                    act.wait_ge(out_sq, outs)
                if t:
                    act.wait_ge(sq_done, b * TT + t)
                act.activation(squares, x_rows[:, t, :].rearrange("p (a n) -> p a n", a=2), ACT.Square,
                               accum_out=ssx[:, t:t + 1])\
                   .then_inc(sq_done, 1)

            def h_high(b, k, banks=BANK_H):
                for k in range(k, k + HP):
                    act.wait_ge(turned, b * KT + k + 1)
                    act.activation(act_hi[:, k, :], ps[:, banks[k], :], ACT.Copy, scale=gpre[:, k:k + 1])\
                       .then_inc(hT_hi, 1)

            def k_high(dst, src):
                for j in range(2):
                    act.activation(dst(j)[0:HD], src[HD * j:HD * j + HD, :], ACT.Copy).then_inc(k_hi, 1)

            def body(b, first, last):
                def q_high(t, hp):
                    s = b * STEPS + t * HP + hp
                    if (t, hp) != (0, 0):
                        act.wait_ge(qk_done, s)
                    for j in range(2):
                        for half in range(2):
                            act.activation(q_parts[HD * half:HD * half + HD, 0, j, :, :],
                                           q[HD * j:HD * j + HD, hp::HP, t * P:t * P + P], ACT.Copy).then_inc(q_hi, 1)

                def exps(t, hp):
                    s = b * STEPS + t * HP + hp
                    par = hp % 2
                    n = t + 1 if first else A_TILES
                    nb = P if first and t == 0 else B_KEYS
                    act.wait_ge(nmax_a, s + 1)
                    for j in range(2):
                        act.activation(pa[:, par, j, 0:n * P], pa[:, par, j, 0:n * P], ACT.Exp, bias=nmax[:, j:j + 1],
                                       accum_out=rsum[:, par, j:j + 1]).then_inc(exp_a, 1)
                    act.wait_ge(nmax_b, s + 1)
                    for j in range(2):
                        keys = slice(B_KEYS - nb, B_KEYS) if j else slice(0, nb)
                        act.activation(pb[:, par, j, keys], pb[:, par, j, keys], ACT.Exp,
                                       bias=nmax[:, 2 + j:3 + j], accum_out=rsum[:, par, 2 + j:3 + j]).then_inc(exp_b, 1)
                    act.wait_ge(sink_arg, s + 1)
                    act.activation(esink[:, :], esink[:, :], ACT.Exp).then_inc(exp_sink, 1)

                def step(i):
                    t, hp = divmod(i - 1, HP)
                    s = b * STEPS + i - 1
                    m = min(t + 1 if first else A_TILES, 4) * P
                    for j in range(2):
                        act.wait_ge(turn[j], s + 1)
                        act.activation(pa[:, hp % 2, j, 0:m], ps[:, BANK_PT[j], 0:m], ACT.Copy).then_inc(pt_ready[j], 1)
                    if i < STEPS:
                        exps(*divmod(i, HP))
                    if i + 1 < STEPS:
                        q_high(*divmod(i + 1, HP))
                    if i == STEPS:
                        act.wait_ge(yt_read, b * (2 * TT) + 2 * TT - 1)
                        for k in range(HP):
                            act.activation(y_a[:, k, :], zx[:, k, :], ACT.Copy).then_inc(yT_hi, 1)
                    act.wait_ge(unit_done, b * UNITS + (U_G + i))
                    if i == STEPS:
                        act.wait_ge(yt_read, b * (2 * TT) + 2 * TT)
                        for k in range(HP, KT):
                            act.activation(act_hi[:, k, :], zx[:, k, :], ACT.Copy).then_inc(yT_hi, 1)
                        split_hi(b, U_M + 1, first)
                    act.activation(gates[:, i - 1, :], ps[:, BANK_G, :], ACT.Tanh, scale=0.5).then_inc(gate_read, 1)
                    if i < STEPS:
                        split_hi(b, U_G + i + 1, first)

                for u in range(U_G):
                    if U_ZA <= u < U_G:
                        act.wait_ge(unit_done, b * UNITS + u + 1)
                        act.activation(zx[:, u - U_ZA, :], ps[:, BANK_T[u % 2], :], ACT.Tanh, scale=0.5)\
                           .then_inc(tanh_done, 1)
                    if u == U_KB:
                        if not first:
                            act.wait_ge(shifted, b * 8)
                        act.wait_ge(unit_done, b * UNITS + u + 1)
                        k_high(lambda j: k_b[:, j, HD:HD + BLK], ps[:, BANK_KB0 if first else BANK_KB, :])
                    if U_KA <= u < U_QA:
                        act.wait_ge(unit_done, b * UNITS + u + 1)
                        k_high(lambda j: k_a[:, 2 * (u - U_KA) + j, BLK:2 * BLK], ps[:, BANK_T[u % 2], :])
                    if u == U_ZA + 2:
                        act.wait_ge(proj_read, b * 26 + U_ZA)
                        q_high(0, 0)
                    split_hi(b, u + 2, first)
                    if u == U_G - 2:
                        q_high(0, 1)
                        exps(0, 0)

                for i in range(1, STEPS + 1):
                    step(i)


                for c in range(KT):
                    split_hi(b, U_M + c + 2, first)
                    act.wait_ge(m_sum, b * KT + c + 1)
                    act.activation(hi_r[:, c, :], pa[:, c % 2, 0, 0:BLK], ACT.Copy).then_inc(m_hi, 1)
                    if c < 2 and not last:
                        for h in range(HP * c, HP * c + HP, 2):
                            act.activation(k_a[:, h:h + 2, 0:BLK], k_a[:, h:h + 2, BLK:2 * BLK], ACT.Copy)\
                               .then_inc(shifted, 1)
                    if c == 6 and not last:
                        act.activation(v_a[:, 0:TT, :], v_a[:, TT:2 * TT, :], ACT.Copy).then_inc(shifted, 1)
                    if c == 7 and not last:
                        act.activation(k_b[:, :, 0:HD], k_b[:, :, BLK:BLK + HD], ACT.Copy).then_inc(shifted, 1)
                        for j in range(2):
                            act.activation(v_bh[HD * j:HD * j + HD, 0, HD * j:HD * j + HD],
                                           v_b[HD:P, TT - 1, HD * j:HD * j + HD], ACT.Copy).then_inc(shifted, 1)
                    if 2 <= c < 6 and not last:
                        x_square(b + 1, c - 2, None if first or c > 2 else b * (2 * TT))

                for u in range(U_O, UNITS):
                    if u + 2 < UNITS:
                        split_hi(b, u + 2, first)
                    elif not last:
                        split_hi(b + 1, u + 2 - UNITS, False)
                    if u == U_O and not last:
                        act.wait_ge(merge_read, b * KT + KT)
                        h_high(b + 1, 0)
                    if u == U_O + 1 and not last:
                        h_high(b + 1, HP)
                    if u == U_O + 3:
                        for t in range(TT):
                            square(b, last, t, 0)
                for t in range(TT):
                    square(b, last, t, 1)

            def square(b, last, t, half):
                n = half * TT + t
                if t < TT - 1:
                    act.wait_ge(row_done, b * (2 * TT - 2) + half * (TT - 1) + t + 1)
                else:
                    act.wait_ge(unit_done, b * UNITS + (U_O + 4 + 4 * half))
                if n >= 2:
                    act.wait_ge(out_sq, b * (2 * TT) + (n - 1))
                else:
                    act.wait_ge(sq_done, b * TT + (TT if last else 2 * TT))
                act.activation(squares[:, n % 2, :], ps[:, half * TT + t, :], ACT.Square,
                               accum_out=ssq[:, half, t:t + 1]).then_inc(out_sq, 1)

            for t in range(TT):
                x_square(0, t, None)
            split_hi(0, 0, True)
            split_hi(0, 1, True)
            act.wait_ge(ready["dma"], 48)
            h_high(0, 0, BANK_H0)
            h_high(0, HP, BANK_H0)
            body(0, True, False)
            with act.Fori(1, NB - 1) as b:
                body(b, False, False)
            body(NB - 1, False, True)

        @block.vector
        def _(dve):
            def split_lo(b, u):
                dve.wait_ge(hi_ready, b * UNITS + (u + 1))
                dve.tensor_tensor(part_unit(w_lo, u), raw_unit(u), as_f32(part_unit(w_hi, u)), ALU.subtract)\
                   .then_inc(lo_ready, 1)

            def refine(n, ts=ALL):
                dve.wait_ge(pow_done, n + 1)
                dve.tensor_tensor(r1[:, ts], r0[:, ts], r0[:, ts], ALU.mult).then_inc(newton, 1)
                dve.wait_ge(newton, n * 4 + 1)
                dve.tensor_tensor(r1[:, ts], r1[:, ts], var[:, ts], ALU.mult).then_inc(newton, 1)
                dve.wait_ge(newton, n * 4 + 2)
                dve.tensor_scalar(r1[:, ts], r1[:, ts], -0.5, 1.5, ALU.mult, ALU.add).then_inc(newton, 1)
                dve.wait_ge(newton, n * 4 + 3)
                dve.tensor_tensor(rstd[:, ts], r1[:, ts], r0[:, ts], ALU.mult).then_inc(newton, 1)
                dve.wait_ge(newton, n * 4 + 4)

            def x_var(b, ts=ALL):
                dve.wait_ge(sq_done, b * TT + ts.stop)
                dve.tensor_scalar(var[:, ts], ssx[:, ts], 1.0 / D, EPS, ALU.mult, ALU.add).then_inc(var_x, 1)

            def x_norm(t):
                dve.tensor_scalar(x_rows[:, t, :], x_rows[:, t, :], rstd[:, t:t + 1], None, ALU.mult)\
                   .then_inc(h_ready, 1)

            def h_low(b, k, banks=BANK_H):
                for k in range(k, k + HP):
                    dve.wait_ge(hT_hi, b * KT + k + 1)
                    dve.scalar_tensor_tensor(out=act_lo[:, k, :], in0=ps[:, banks[k], :], scalar=gpre[:, k:k + 1],
                                             in1=as_f32(act_hi[:, k, :]), op0=ALU.mult, op1=ALU.subtract)\
                       .then_inc(hT_lo, 1)

            def add_rows(b, t):
                if t % 2 == 0:
                    dve.wait_ge(weighed, b * (2 * TT) + TT + t + 2)
                    dve.wait_ge(res_full, b * (16 * TT) + 16 * TT)
                dve.scalar_tensor_tensor(out=out_rows[:, t, :], in0=out_rows[:, t, :], scalar=rstd[:, t:t + 1],
                                         in1=x_rows[:, t, :], op0=ALU.mult, op1=ALU.add).then_inc(added, 1)

            def body(b, first, last):
                def scores_of(t, hp):
                    s = b * STEPS + t * HP + hp
                    par = hp % 2
                    n = t + 1 if first else A_TILES
                    b0 = CHUNK if first and t == 0 else 0
                    dve.wait_ge(qk_done, s + 1)
                    for j in range(2):
                        slope = 2.0 ** (-8.0 / NH * (hp + HP * j + 1))
                        pieces = [(b0, b0, B_KEYS)] if j else [(0, CHUNK, B_KEYS)] + ([] if b0 else [(P, 0, CHUNK)])
                        for at, lo, hi in pieces:
                            o = dve.scalar_tensor_tensor(
                                out=pb[:, par, j, at:at + hi - lo], in0=dist_b[:, lo:hi], scalar=-slope,
                                in1=scores[j][:, P + A_KEYS + lo:P + A_KEYS + hi], op0=ALU.mult, op1=ALU.add)
                        o.then_inc(biased_b, 1)
                    for j in range(2):
                        dve.tensor_tensor_reduce(pa[:, par, j, 0:n * P], scores[j][:, P:P + n * P],
                                                 bias_a[:, 2 * hp + j, A_KEYS - n * P:A_KEYS], 1.0, -3e38,
                                                 ALU.add, ALU.max, rmax[:, j:j + 1]).then_inc(scores_read, 1)
                    dve.wait_ge(scores_read, s * 2 + 2)
                    dve.tensor_scalar(nmax[:, 0:2], rmax[:, 0:2], -1.0, None, ALU.mult).then_inc(nmax_a, 1)
                    dve.wait_ge(biased_b, s * 2 + 2)
                    dve.tensor_reduce(rmax[:, 2:4], b_thirds(par)[:, 0:3:2, :] if b0 else pb[:, par, :, :],
                                      AX.X, ALU.max).then_inc(max_b, 1)
                    dve.wait_ge(max_b, s + 1)
                    dve.scalar_tensor_tensor(out=nmax[:, 2:4], in0=rmax[:, 2:4], scalar=-1.0, in1=nsink[:, :, hp],
                                             op0=ALU.mult, op1=ALU.min).then_inc(nmax_b, 1)
                    dve.wait_ge(nmax_b, s + 1)
                    dve.tensor_tensor(esink[:, :], sink[:, :, hp], nmax[:, 2:4], ALU.add).then_inc(sink_arg, 1)

                def values_of(t, hp):
                    s = b * STEPS + t * HP + hp
                    par = hp % 2
                    if not first:
                        dve.wait_ge(turn[2], s - STEPS + 1)
                        dve.tensor_copy(pa[:, par, :, 4 * P:5 * P],
                                        ps[:, BANK_PT[0], 0:2 * P].rearrange("p (j n) -> p j n", j=2))\
                           .then_inc(pt_ready[2], 1)
                    dve.wait_ge(turn[3], s + 1)
                    step3 = slice(0, 3, 2) if first and t == 0 else slice(0, 3)
                    dve.tensor_copy(b_thirds(par)[:, step3, :],
                                    ps[:, BANK_PT[1], 0:3 * P].rearrange("p (a n) -> p a n", n=P)[:, step3, :])\
                       .then_inc(pt_ready[3], 1)
                    if t * HP + hp + 2 < STEPS:
                        q_low(*divmod(t * HP + hp + 2, HP))
                    dve.wait_ge(inv_ready, s + 1)
                    dve.wait_ge(pv_done, s + 1)
                    acc = ps[:, BANK_Y, 0:4 * HD].rearrange("p (h d) -> p h d", d=HD)
                    for br in range(2):
                        y = dve.tensor_tensor(q[:, br * HP + hp, t * P:t * P + P].rearrange("p (j d) -> p j d", j=2),
                                              acc[:, 2 * br:2 * br + 2, :],
                                              rinv[:, 2 * br:2 * br + 2].unsqueeze(2).broadcast_to([P, 2, HD]), ALU.mult)
                    y.then_inc(y_ready, 1)

                def q_low(t, hp):
                    s = b * STEPS + t * HP + hp
                    dve.wait_ge(q_hi, s * 4 + 4)
                    for j in range(2):
                        rows_j = slice(HD * j, HD * j + HD)
                        dve.tensor_tensor(q_parts[0:HD, 1, j, :, :], q[rows_j, hp::HP, t * P:t * P + P],
                                          as_f32(q_parts[rows_j, 0, j, :, :]), ALU.subtract).then_inc(q_lo, 1)

                def k_low(n, dst, src):
                    dve.wait_ge(k_hi, b * (2 * TT + 2) + 2 * n + 2)
                    for j in range(2):
                        o = dve.tensor_tensor(dst(j)[HD:P], src[HD * j:HD * j + HD, :], as_f32(dst(j)[0:HD]),
                                              ALU.subtract)
                    return o

                def inverse_of(t, hp):
                    s = b * STEPS + t * HP + hp
                    par = hp % 2
                    dve.wait_ge(exp_sink, s + 1)
                    dve.tensor_tensor(rsum[:, par, 2:4], rsum[:, par, 2:4], esink[:, :], ALU.add).then_inc(sum_b, 1)
                    dve.wait_ge(sum_b, s + 1)
                    dve.reciprocal(rinv[:, :], rsum[:, par, :]).then_inc(inv_ready, 1)

                def gate_y(t):
                    for br in range(2):
                        z_t = zx[:, br * HP:br * HP + HP, t * P:t * P + P]
                        dve.wait_ge(yt_done, b * (2 * TT) + (t * 2 + br + 1))
                        dve.tensor_tensor(z_t, ps[:, BANK_PT[br], :].rearrange("p (k n) -> p k n", k=HP), z_t, ALU.mult)\
                           .then_inc(yt_read, 1)

                va, kb, vb = (BANK_VA0, BANK_KB0, BANK_VB0) if first else (BANK_VA, BANK_KB, BANK_VB)
                for u in range(U_G):
                    if u >= U_VB:
                        dve.wait_ge(unit_done, b * UNITS + u + 1)
                    bank = ps[:, BANK_T[u % 2], :]
                    if u == U_VB:
                        dve.tensor_copy(pa[:, 0, 0, 0:BLK], ps[:, vb, :]).then_inc(v_staged, 1)
                    elif u == U_KB:
                        k_low(0, lambda j: k_b[:, j, HD:HD + BLK], ps[:, kb, :]).then_inc(proj_read, 1)
                    elif U_KA <= u < U_QA:
                        k_low(1 + u - U_KA, lambda j: k_a[:, 2 * (u - U_KA) + j, BLK:2 * BLK], bank).then_inc(proj_read, 1)
                    elif U_QA <= u < U_ZA:
                        if not first and u == U_QA:
                            dve.wait_ge(stored, b * (16 * TT))
                        dve.tensor_scalar(q[:, u - U_QA, :], bank, HD ** -0.5, None, ALU.mult).then_inc(proj_read, 1)
                    elif u >= U_ZA:
                        n = u - U_ZA
                        dve.wait_ge(tanh_done, b * KT + n + 1)
                        dve.scalar_tensor_tensor(out=zx[:, n, :], in0=zx[:, n, :], scalar=1.0, in1=bank,
                                                 op0=ALU.add, op1=ALU.mult).then_inc(proj_read, 1)
                    split_lo(b, u + 2)
                    if u < TT and not first:
                        if u == 0:
                            refine(2 * b + 1)
                        add_rows(b - 1, u)
                    if u == U_ZA + 2:
                        q_low(0, 0)
                    if u == U_KB:
                        dve.wait_ge(v_turned, b + 1)
                        if first:
                            dve.wait_ge(ready["v_bh"], 1)
                        if not first:
                            dve.wait_ge(shifted, b * 8)
                        v_rows = ps[:, vb, :].rearrange("p (t c) -> p t c", t=TT)
                        for j in range(2):
                            dve.tensor_copy(v_bh[HD * j:HD * j + HD, 1:TT, HD * j:HD * j + HD],
                                            v_rows[HD:P, 0:TT - 1, HD * j:HD * j + HD])
                        dve.tensor_copy(v_b[:, :, :], v_rows).then_inc(proj_read, 1)
                    if u == U_G - 2:
                        if first:
                            dve.wait_ge(ready["mask"], 4)
                        scores_of(0, 0)
                        q_low(0, 1)
                    if u == U_VA + 3:
                        dve.wait_ge(unit_done, b * UNITS + u + 1)
                        if not first:
                            dve.wait_ge(shifted, b * 8)
                        for t in range(TT):
                            dve.tensor_copy(v_a[:, TT + t, :], ps[:, va[t], :]).then_inc(proj_read, 1)

                for i in range(1, STEPS + 1):
                    t, hp = divmod(i - 1, HP)
                    inverse_of(t, hp)
                    if i < STEPS:
                        scores_of(*divmod(i, HP))
                    values_of(t, hp)
                    if hp == HP - 1:
                        gate_y(t)
                    if i < STEPS:
                        split_lo(b, U_G + i + 1)

                for k in range(KT):
                    dve.wait_ge(yT_hi, b * KT + k + 1)
                    hi, lo = (y_a[:, k, :], y_a[:, HP + k, :]) if k < HP else (act_hi[:, k, :], act_lo[:, k, :])
                    dve.tensor_tensor(lo, zx[:, k, :], as_f32(hi), ALU.subtract).then_inc(yT_lo, 1)
                split_lo(b, U_M + 1)

                b_side = pb[:, :, :, :].rearrange("p a j n -> p (a j n)")[:, 0:BLK]
                for c in range(KT):
                    m = pa[:, c % 2, 0, 0:BLK]
                    dve.wait_ge(unit_done, b * UNITS + U_M + c + 1)
                    dve.scalar_tensor_tensor(out=m, in0=gates[:, c, :], scalar=1.0, in1=ps[:, 2 * (c % 2), :],
                                             op0=ALU.add, op1=ALU.mult)
                    dve.scalar_tensor_tensor(out=b_side, in0=gates[:, KT + c, :], scalar=1.0,
                                             in1=ps[:, 2 * (c % 2) + 1, :], op0=ALU.add, op1=ALU.mult)\
                       .then_inc(merge_read, 1)
                    split_lo(b, U_M + c + 2)
                    dve.wait_ge(merge_read, b * KT + c + 1)
                    dve.tensor_tensor(m, m, b_side, ALU.add).then_inc(m_sum, 1)
                    dve.wait_ge(m_hi, b * KT + c + 1)
                    dve.tensor_tensor(lo_r[:, c, :], m, as_f32(hi_r[:, c, :]), ALU.subtract).then_inc(m_lo, 1)
                    if c == 5 and not last:
                        x_var(b + 1)
                    if c == 6 and not last:
                        refine(2 * b + 2)
                        x_norm(0)
                    if c == 7 and not last:
                        x_norm(1)

                def weigh(t, half):
                    dve.wait_ge(out_sq, b * (2 * TT) + (half * TT + t + 1))
                    dve.tensor_tensor(out_rows[:, t, half * 512:half * 512 + 512], ps[:, half * TT + t, :],
                                      gpost[:, half * 512:half * 512 + 512], ALU.mult).then_inc(weighed, 1)

                for u in range(U_O, UNITS):
                    if u + 2 < UNITS:
                        split_lo(b, u + 2)
                    elif not last:
                        split_lo(b + 1, u + 2 - UNITS)
                    if u == U_O and not last:
                        x_norm(2)
                        x_norm(3)
                        h_low(b + 1, 0)
                    if u == U_O + 1 and not last:
                        h_low(b + 1, HP)
                    if u == U_O + 3:
                        for t in range(TT):
                            weigh(t, 0)
                def row_var(n, ts):
                    dve.tensor_tensor(ssq[:, 0, ts], ssq[:, 0, ts], ssq[:, 1, ts], ALU.add).then_inc(sq_sum, 1)
                    dve.wait_ge(sq_sum, n + 1)
                    dve.tensor_scalar(var[:, ts], ssq[:, 0, ts], 1.0 / D, 16 * EPS, ALU.mult, ALU.add).then_inc(var_o, 1)

                if not last:
                    for t in range(TT):
                        weigh(t, 1)
                    row_var(b, ALL)
                else:
                    for g, ts in enumerate(PAIRS):
                        for t in range(ts.start, ts.stop):
                            weigh(t, 1)
                        row_var(b + g, ts)
                        refine(2 * b + 2 + g, ts)
                        for t in range(ts.start, ts.stop):
                            add_rows(b, t)

            for g, ts in enumerate(PAIRS):
                x_var(0, ts)
                refine(g, ts)
                for t in range(ts.start, ts.stop):
                    x_norm(t)
            split_lo(0, 0)
            dve.wait_ge(ready["dma"], 48)
            h_low(0, 0, BANK_H0)
            split_lo(0, 1)
            h_low(0, HP, BANK_H0)
            dve.tensor_scalar(nsink[:, :, :], sink[:, :, :], -1.0, None, ALU.mult).then_inc(ready["nsink"], 1)
            far = REL_ROW - REL_NEAR
            rel_row = gates[0:NH, 0:2, :].rearrange("p a n -> p (a n)")
            dve.wait_ge(ready["rel"], 16)
            dve.tensor_copy(rel_row[:, 0:far], pa[0:NH, 0, 0, REL - 1:REL].broadcast_to([NH, far])).then_inc(ready["relrow"], 1)
            dve.tensor_copy(rel_row[:, far:REL_ROW], pa[0:NH, 0, 0, REL - REL_NEAR:REL][:, ::-1]).then_inc(ready["relrow"], 1)
            dve.wait_ge(ready["dist0"], 1)
            dve.scalar_tensor_tensor(out=dist_b[:, :], in0=dist_b[:, :], scalar=-1.0, in1=dist_b[:, :],
                                     op0=ALU.mult, op1=ALU.max).then_inc(ready["dist1"], 1)
            dve.wait_ge(ready["nsink"], 1)
            body(0, True, False)
            with dve.Fori(1, NB - 1) as b:
                body(b, False, False)
            body(NB - 1, False, True)

        @block.tensor
        def _(pe):
            def three(out_ap, lhs, rhs, start, stop):
                (lh, ll), (rh, rl) = lhs, rhs
                pe.matmul(out_ap, lh, rh, start=start, stop=False)
                pe.matmul(out_ap, lh, rl, start=False, stop=False)
                return pe.matmul(out_ap, ll, rh, start=False, stop=stop)

            def w_tile(slot, k):
                return cols(w_hi, slot)[:, k, :], cols(w_lo, slot)[:, k, :]

            def w_row(slot, k):
                return rows(w_hi, slot)[:, k, :], rows(w_lo, slot)[:, k, :]

            def a_cols(k):
                return act_hi[:, k, :], act_lo[:, k, :]

            def y_cols(k):
                if k < HP:
                    return y_a[:, k, :], y_a[:, HP + k, :]
                return a_cols(k)

            def a_tile(k, t):
                return act_hi[:, k, t * P:t * P + P], act_lo[:, k, t * P:t * P + P]

            def m_tile(k, t):
                return hi_r[:, k, t * P:t * P + P], lo_r[:, k, t * P:t * P + P]

            def turn_h(b, k, banks=BANK_H):
                if k and banks == BANK_H:
                    pe.wait_ge(hT_lo, b * KT + k)
                for t in range(TT):
                    if not k:
                        pe.wait_ge(h_ready, b * TT + t + 1)
                    for i in range(k, k + HP):
                        m = pe.transpose(ps[:, banks[i], t * P:t * P + P], x_rows[:, t, i * P:i * P + P], ident[:, :])
                        if t == TT - 1:
                            m.then_inc(turned, 1)

            def body(b, first, last):
                va, kb, vb = (BANK_VA0, BANK_KB0, BANK_VB0) if first else (BANK_VA, BANK_KB, BANK_VB)
                if not first:
                    pe.wait_ge(weighed, b * (2 * TT) - TT)
                for u in range(U_VA, U_VB):
                    pe.wait_ge(lo_ready, b * UNITS + u + 1)
                    if first:
                        pe.wait_ge(hT_lo, max(HP, 2 * u + 2))
                    for t in range(TT):
                        for i in range(2):
                            k = 2 * u + i
                            m = three(ps[:, va[t], :], a_tile(k, t), w_row(u % 2, i), k == 0, k == KT - 1)
                    m.then_inc(unit_done, 1)
                if not first:
                    pe.wait_ge(weighed, b * (2 * TT))
                for u, bank in (U_VB, vb), (U_KB, kb):
                    pe.wait_ge(lo_ready, b * UNITS + u + 1)
                    for k in range(KT):
                        m = three(ps[:, bank, :], w_tile(u % 2, k), a_cols(k), k == 0, k == KT - 1)
                    m.then_inc(unit_done, 1)
                pe.wait_ge(v_staged, b + 1)
                for t in range(TT):
                    m = pe.transpose(ps[:, vb, t * P:t * P + P], pa[:, 0, 0, t * P:t * P + P], ident[:, :])
                m.then_inc(v_turned, 1)

                def column_unit(u, j):
                    pe.wait_ge(lo_ready, u + 1)
                    for k in range(KT):
                        m = three(ps[:, BANK_T[j], :], w_tile(j, k), a_cols(k), k == 0, k == KT - 1)
                    m.then_inc(unit_done, 1)

                if first:
                    pe.wait_ge(proj_read, TT)
                for j in range(2):
                    column_unit(b * UNITS + (U_KA + j), j)
                with pe.Fori(1, (U_G - U_KA) // 2 - 1) as i:
                    for j in range(2):
                        pe.wait_ge(proj_read, b * 26 + i * 2 + (U_KA + j - 1))
                        column_unit(b * UNITS + i * 2 + (U_KA + j), j)

                def gate_part(hp, ks):
                    for k in ks:
                        m = three(ps[:, BANK_G, :], w_tile(hp % 2, k), a_cols(k), k == 0, k == KT - 1)
                    return m

                def scores_of(t, hp):
                    s = b * STEPS + t * HP + hp
                    n = t + 1 if first else A_TILES
                    k0 = (TT + t - (n - 1)) * P
                    if (t, hp) != (0, 0):
                        pe.wait_ge(scores_read, s * 2)
                    pe.wait_ge(q_lo, s * 2 + 2)
                    for j in range(2):
                        b0 = CHUNK if first and t == 0 else 0
                        for br, head, c0, m0, m1 in ((0, k_a[:, 2 * hp + j, :], k0, P, min(n, 3) * P),
                                                     (0, k_a[:, 2 * hp + j, :], k0 + 3 * P, 4 * P, (n - 3) * P),
                                                     (1, k_b[:, j, :], t * P + b0, P + A_KEYS + b0, B_KEYS - b0)):
                            if m1 <= 0:
                                continue
                            pe.matmul(scores[j][:, m0:m0 + m1], q_parts[:, 0, j, br, :], head[:, c0:c0 + m1],
                                      start=True, stop=False)
                            m = pe.matmul(scores[j][:, m0:m0 + m1], q_parts[0:HD, 1, j, br, :], head[0:HD, c0:c0 + m1],
                                          start=False, stop=True)
                    m.then_inc(qk_done, 1)

                def step(i):
                    t, hp = divmod(i - 1, HP)
                    s = b * STEPS + i - 1
                    par = hp % 2
                    n = t + 1 if first else A_TILES
                    whole = not (first and t == 0)
                    ks = (0, 3, 4, 5, 8) if i == STEPS else (2, 4, 6, 8, 8) if hp == HP - 1 else (2, 4, 7, 8, 8)

                    def gate_wait():
                        pe.wait_ge(lo_ready, b * UNITS + (U_G + i))
                        if i == 1:
                            pe.wait_ge(proj_read, b * 26 + 25)
                        else:
                            pe.wait_ge(gate_read, s)

                    if i < STEPS:
                        scores_of(*divmod(i, HP))
                    if ks[0]:
                        gate_wait()
                        gate_part(hp, range(0, ks[0]))
                    for j in range(2):
                        pe.wait_ge(exp_a, s * 2 + (j + 1))
                        if hp == 0 and not (first and t == 0):
                            pe.wait_ge(yt_read, b * (2 * TT) + (t * 2 - (1 - j)))
                        for x in range(min(n, 4)):
                            m = pe.transpose(ps[:, BANK_PT[j], x * P:x * P + P], pa[:, par, j, x * P:x * P + P], ident[:, :])
                        m.then_inc(turn[j], 1)
                    if not ks[0]:
                        gate_wait()
                    gate_part(hp, range(ks[0], ks[1]))
                    pe.wait_ge(pt_ready[0], s + 1)
                    if n == A_TILES:
                        for j in range(2):
                            m = pe.transpose(ps[:, BANK_PT[0], j * P:j * P + P], pa[:, par, j, 4 * P:5 * P], ident[:, :])
                        m.then_inc(turn[2], 1)
                    pe.wait_ge(pt_ready[1], s + 1)
                    pe.wait_ge(exp_b, s * 2 + 2)
                    for x in range(3) if whole else (0, 2):
                        m = pe.transpose(ps[:, BANK_PT[1], x * P:x * P + P], b_thirds(par)[:, x, :], ident[:, :])
                    m.then_inc(turn[3], 1)
                    gate_part(hp, range(ks[1], ks[2]))

                    if i > 1:
                        pe.wait_ge(y_ready, s)
                    else:
                        pe.wait_ge(proj_read, b * 26 + 26)
                    v0 = TT + t - (n - 1)
                    if n == A_TILES:
                        pe.wait_ge(pt_ready[2], s - STEPS + 1)
                    for j in range(2):
                        for x in range(n):
                            pe.matmul(ps[:, BANK_Y, j * HD:j * HD + HD], pa[:, par, j, x * P:x * P + P],
                                      v_a[:, v0 + x, (2 * hp + j) * HD:(2 * hp + j + 1) * HD],
                                      start=(x == 0), stop=(x == n - 1))
                    pe.wait_ge(pt_ready[3], s + 1)
                    pt = b_thirds(par)
                    if whole:
                        pe.matmul(ps[:, BANK_Y, 2 * HD:4 * HD], pt[:, 1, :], v_bh[:, t, :], start=True, stop=False)
                    for j in range(2):
                        m = pe.matmul(ps[:, BANK_Y, (2 + j) * HD:(3 + j) * HD], pt[:, 2 * j, :],
                                      v_b[:, t, j * HD:j * HD + HD], start=not whole,
                                      stop=j == 1 or not whole)
                    m.then_inc(pv_done, 1)
                    m = gate_part(hp, range(ks[2], ks[3]))
                    if i < STEPS:
                        m.then_inc(unit_done, 1)

                    if hp == HP - 1:
                        pe.wait_ge(y_ready, s + 1)
                        for br in range(2):
                            for x in range(HP):
                                m = pe.transpose(ps[:, BANK_PT[br], x * P:x * P + P],
                                                 q[:, br * HP + x, t * P:t * P + P], ident[:, :])
                            m.then_inc(yt_done, 1)
                    if i == STEPS:
                        gate_part(hp, range(ks[3], ks[4])).then_inc(unit_done, 1)

                pe.wait_ge(proj_read, b * 26 + (U_G - 3))
                column_unit(b * UNITS + (U_G - 2), 0)
                scores_of(0, 0)
                pe.wait_ge(proj_read, b * 26 + (U_G - 2))
                column_unit(b * UNITS + (U_G - 1), 1)
                for i in range(1, STEPS + 1):
                    step(i)

                pe.wait_ge(scores_read, (b * STEPS + STEPS) * 2)
                for c in range(KT):
                    pe.wait_ge(lo_ready, b * UNITS + U_M + c + 1)
                    if c >= 2:
                        pe.wait_ge(merge_read, b * KT + c - 1)
                    for br in range(2):
                        for i in range(HP):
                            k = br * HP + i
                            if c == 0:
                                pe.wait_ge(yT_lo, b * KT + k + 1)
                            m = three(ps[:, 2 * (c % 2) + br, :], w_tile(c % 2, k), y_cols(k), i == 0, i == HP - 1)
                    m.then_inc(unit_done, 1)

                for u in range(U_O, UNITS):
                    half, i0 = (u - U_O) // 4, (u - U_O) % 4
                    pe.wait_ge(lo_ready, b * UNITS + u + 1)
                    if half == 0:
                        pe.wait_ge(m_lo, b * KT + 2 * i0 + 2)
                    if u == U_O + 4 and not last:
                        pe.wait_ge(hT_lo, b * KT + 2 * KT)
                    for t in range(TT):
                        if u == U_O and t % 2 == 0:
                            pe.wait_ge(merge_read, b * KT + KT - 1 + t // 2)
                        for i in range(2):
                            k = 2 * i0 + i
                            m = three(ps[:, half * TT + t, :], m_tile(k, t), w_row(u % 2, i), k == 0, k == KT - 1)
                        if i0 == 3 and t < TT - 1:
                            m.then_inc(row_done, 1)
                    m.then_inc(unit_done, 1)
                    if u == U_O + 1 and not last:
                        pe.wait_ge(gate_read, b * STEPS + STEPS)
                        turn_h(b + 1, 0)
                    if u == U_O + 2 and not last:
                        turn_h(b + 1, HP)

            pe.wait_ge(ready["ident"], 1)
            turn_h(0, 0, BANK_H0)
            turn_h(0, HP, BANK_H0)
            body(0, True, False)
            with pe.Fori(1, NB - 1) as b:
                body(b, False, False)
            body(NB - 1, False, True)


_INS = ["x", "g_pre", "w_in", "rel_bias", "sinks", "w_branch_a", "w_branch_b", "w_out", "g_post"]


def kernel(**inputs):
    import numpy as _np
    import concourse.bacc as _bacc
    from concourse import mybir as _mybir
    from concourse.bass_utils import run_bass_kernel_spmd as _run

    nc = _bacc.Bacc("TRN2", target_bir_lowering=False, num_devices=1, dynamic_dma_scratch_size=1024)
    arrays, args = {}, []
    for name in _INS:
        a = _np.ascontiguousarray(inputs[name])
        arrays[f"in_{name}"] = a
        args.append(nc.dram_tensor(f"in_{name}", a.shape, _mybir.dt.from_np(a.dtype), kind="ExternalInput").ap())
    shape = tuple(inputs["x"].shape)
    args.append(nc.dram_tensor("out_x", shape, F32, kind="ExternalOutput").ap())
    build_block(nc, *args)
    r = _run(nc, [arrays], core_ids=[0])
    return r.results[0]["out_x"]
```
